# Optimizing a Trainium2 kernel written in Bass

```python
import jax, jax.numpy as jnp
from jax import lax
import numpy as np

D_MODEL = 2048
BATCH = 1
SEQ = 256
DEPTH = 2

CHUNK = 64
Q_BLOCK = 128
N_MIXERS = 2
N_MLA_LAYERS = (DEPTH + 1) // 2
N_FOX_LAYERS = DEPTH // 2

MLA_HEADS = 16
MLA_Q_LORA = 512
MLA_KV_LORA = 512
MLA_NOPE_DIM = 128
MLA_ROPE_DIM = 64
MLA_V_DIM = 128
ROPE_THETA = 10000.0

FOX_HEADS = 16
FOX_HEAD_DIM = D_MODEL // FOX_HEADS

D_FF = -(-8 * D_MODEL // (3 * 256)) * 256

DEEPNORM_ALPHA = (2 * DEPTH) ** 0.25
DEEPNORM_BETA = (8 * DEPTH) ** -0.25
LN_EPS = 1e-5
RMS_EPS = 1e-6

kernel_name = "hybrid_mla_fox_deepnorm_adaln_trunk"

def _layer_norm(x, g, b):
    xf = x.astype(jnp.float32)
    mu = jnp.mean(xf, axis=-1, keepdims=True)
    var = jnp.mean(jnp.square(xf - mu), axis=-1, keepdims=True)
    y = (xf - mu) * lax.rsqrt(var + LN_EPS)
    return (y * g.astype(jnp.float32) + b.astype(jnp.float32)).astype(x.dtype)

def _rms_norm(x, g):
    xf = x.astype(jnp.float32)
    y = xf * lax.rsqrt(jnp.mean(jnp.square(xf), axis=-1, keepdims=True) + RMS_EPS)
    return (y * g.astype(jnp.float32)).astype(x.dtype)

def _rope_cos_sin(positions, dtype):
    inv_freq = ROPE_THETA ** (-jnp.arange(0, MLA_ROPE_DIM, 2, dtype=jnp.float32) / MLA_ROPE_DIM)
    ang = positions.astype(jnp.float32)[..., None] * inv_freq
    return jnp.cos(ang).astype(dtype), jnp.sin(ang).astype(dtype)

def _rope(x, cos, sin):
    x2 = x.reshape(*x.shape[:-1], MLA_ROPE_DIM // 2, 2)
    x0, x1 = x2[..., 0], x2[..., 1]
    out = jnp.stack([x0 * cos - x1 * sin, x0 * sin + x1 * cos], axis=-1)
    return out.reshape(x.shape)

def _mla(h, positions, w_down, q_norm, w_uq, kv_norm, w_uk, w_uv, w_o):
    B, S, _ = h.shape
    H = MLA_HEADS
    lat = h @ w_down
    q_lat, kv_lat, k_pe = jnp.split(lat, [MLA_Q_LORA, MLA_Q_LORA + MLA_KV_LORA], axis=-1)
    q = (_rms_norm(q_lat, q_norm) @ w_uq).reshape(B, S, H, MLA_NOPE_DIM + MLA_ROPE_DIM)
    q_nope, q_pe = q[..., :MLA_NOPE_DIM], q[..., MLA_NOPE_DIM:]
    cos, sin = _rope_cos_sin(positions, h.dtype)
    q_pe = _rope(q_pe, cos[:, :, None, :], sin[:, :, None, :])
    k_pe = _rope(k_pe, cos, sin)
    c_kv = _rms_norm(kv_lat, kv_norm)
    k_nope = (c_kv @ w_uk).reshape(B, S, H, MLA_NOPE_DIM)
    v = (c_kv @ w_uv).reshape(B, S, H, MLA_V_DIM)
    scale = (MLA_NOPE_DIM + MLA_ROPE_DIM) ** -0.5
    chunk_id = jnp.arange(S) // CHUNK
    outs = []
    for qs in range(0, S, Q_BLOCK):
        ke = qs + Q_BLOCK
        s = (jnp.einsum('bqhd,bkhd->bhqk', q_nope[:, qs:ke], k_nope[:, :ke])
             + jnp.einsum('bqhr,bkr->bhqk', q_pe[:, qs:ke], k_pe[:, :ke])).astype(jnp.float32) * scale
        mask = chunk_id[qs:ke, None] >= chunk_id[None, :ke]
        p = jax.nn.softmax(jnp.where(mask, s, -jnp.inf), axis=-1).astype(v.dtype)
        outs.append(jnp.einsum('bhqk,bkhd->bqhd', p, v[:, :ke]))
    o = jnp.concatenate(outs, axis=1).reshape(B, S, H * MLA_V_DIM)
    return o @ w_o

def _fox(h, w_in, b_f, w_o):
    B, S, D = h.shape
    H, Dh = FOX_HEADS, FOX_HEAD_DIM
    proj = h @ w_in
    q, k, v, f_logit = jnp.split(proj, [D, 2 * D, 3 * D], axis=-1)
    q = q.reshape(B, S, H, Dh)
    k = k.reshape(B, S, H, Dh)
    v = v.reshape(B, S, H, Dh)
    log_f = jax.nn.log_sigmoid((f_logit + b_f).astype(jnp.float32))
    cum = jnp.transpose(lax.cumsum(log_f, axis=1), (0, 2, 1))
    scale = Dh ** -0.5
    pos = jnp.arange(S)
    outs = []
    for qs in range(0, S, Q_BLOCK):
        ke = qs + Q_BLOCK
        s = jnp.einsum('bqhd,bkhd->bhqk', q[:, qs:ke], k[:, :ke]).astype(jnp.float32) * scale
        s = s + cum[:, :, qs:ke, None] - cum[:, :, None, :ke]
        mask = pos[qs:ke, None] >= pos[None, :ke]
        p = jax.nn.softmax(jnp.where(mask, s, -jnp.inf), axis=-1).astype(v.dtype)
        outs.append(jnp.einsum('bhqk,bkhd->bqhd', p, v[:, :ke]))
    o = jnp.concatenate(outs, axis=1).reshape(B, S, D)
    return o @ w_o

def _swiglu(h, w1, w3, w2):
    return (jax.nn.silu(h @ w1) * (h @ w3)) @ w2

def _dense(key, shape, fan_in, scale=1.0):
    return jax.random.normal(key, shape, jnp.float32) * (scale * fan_in ** -0.5)

def setup_inputs(seed: int = 0) -> dict:
    key = jax.random.key(seed)
    ks = jax.random.split(key, 32)
    D, L, NA, NB = D_MODEL, DEPTH, N_MLA_LAYERS, N_FOX_LAYERS
    HA, HB = MLA_HEADS, FOX_HEADS
    x = jax.random.normal(ks[0], (BATCH, SEQ, D), jnp.float32)
    c = jax.random.normal(ks[1], (BATCH, D), jnp.float32)
    offset = jax.random.randint(ks[2], (BATCH, 1), 0, 16, dtype=jnp.int32) * CHUNK
    positions = offset + jnp.arange(SEQ, dtype=jnp.int32)[None, :]

    ada_w = _dense(ks[3], (L, D, 6 * D), D, 0.5)
    ada_b = 0.01 * jax.random.normal(ks[4], (L, 6 * D), jnp.float32)
    ln1_g = 1.0 + 0.02 * jax.random.normal(ks[5], (L, D), jnp.float32)
    ln1_b = 0.02 * jax.random.normal(ks[6], (L, D), jnp.float32)
    ln2_g = 1.0 + 0.02 * jax.random.normal(ks[7], (L, D), jnp.float32)
    ln2_b = 0.02 * jax.random.normal(ks[8], (L, D), jnp.float32)
    ffn_w1 = _dense(ks[9], (L, D, D_FF), D)
    ffn_w3 = _dense(ks[10], (L, D, D_FF), D)
    ffn_w2 = _dense(ks[11], (L, D_FF, D), D_FF, DEEPNORM_BETA)

    mla_w_down = _dense(ks[12], (NA, D, MLA_Q_LORA + MLA_KV_LORA + MLA_ROPE_DIM), D)
    mla_q_norm = 1.0 + 0.02 * jax.random.normal(ks[13], (NA, MLA_Q_LORA), jnp.float32)
    mla_w_uq = _dense(ks[14], (NA, MLA_Q_LORA, HA * (MLA_NOPE_DIM + MLA_ROPE_DIM)), MLA_Q_LORA)
    mla_kv_norm = 1.0 + 0.02 * jax.random.normal(ks[15], (NA, MLA_KV_LORA), jnp.float32)
    mla_w_uk = _dense(ks[16], (NA, MLA_KV_LORA, HA * MLA_NOPE_DIM), MLA_KV_LORA)
    mla_w_uv = _dense(ks[17], (NA, MLA_KV_LORA, HA * MLA_V_DIM), MLA_KV_LORA, DEEPNORM_BETA)
    mla_w_o = _dense(ks[18], (NA, HA * MLA_V_DIM, D), HA * MLA_V_DIM, DEEPNORM_BETA)

    fox_wq = _dense(ks[19], (NB, D, D), D)
    fox_wk = _dense(ks[20], (NB, D, D), D)
    fox_wv = _dense(ks[21], (NB, D, D), D, DEEPNORM_BETA)
    fox_wf = _dense(ks[22], (NB, D, HB), D)
    fox_w_in = jnp.concatenate([fox_wq, fox_wk, fox_wv, fox_wf], axis=-1)
    fox_b_f = jax.random.uniform(ks[23], (NB, HB), jnp.float32, 1.0, 4.0)
    fox_w_o = _dense(ks[24], (NB, D, D), D, DEEPNORM_BETA)

    return {
        "x": x, "c": c, "positions": positions,
        "ada_w": ada_w, "ada_b": ada_b,
        "ln1_g": ln1_g, "ln1_b": ln1_b, "ln2_g": ln2_g, "ln2_b": ln2_b,
        "ffn_w1": ffn_w1, "ffn_w3": ffn_w3, "ffn_w2": ffn_w2,
        "mla_w_down": mla_w_down, "mla_q_norm": mla_q_norm, "mla_w_uq": mla_w_uq,
        "mla_kv_norm": mla_kv_norm, "mla_w_uk": mla_w_uk, "mla_w_uv": mla_w_uv, "mla_w_o": mla_w_o,
        "fox_w_in": fox_w_in, "fox_b_f": fox_b_f, "fox_w_o": fox_w_o,
    }

def reference(x, c, positions, ada_w, ada_b, ln1_g, ln1_b, ln2_g, ln2_b,
              ffn_w1, ffn_w3, ffn_w2,
              mla_w_down, mla_q_norm, mla_w_uq, mla_kv_norm, mla_w_uk, mla_w_uv, mla_w_o,
              fox_w_in, fox_b_f, fox_w_o):
    c_act = jax.nn.silu(c)
    for i in range(DEPTH):
        mod = c_act @ ada_w[i] + ada_b[i]
        sh_a, sc_a, g_a, sh_f, sc_f, g_f = [m[:, None, :] for m in jnp.split(mod, 6, axis=-1)]

        h = x * (1.0 + sc_a) + sh_a
        j = i // N_MIXERS
        if i % N_MIXERS == 0:
            y = _mla(h, positions, mla_w_down[j], mla_q_norm[j], mla_w_uq[j],
                     mla_kv_norm[j], mla_w_uk[j], mla_w_uv[j], mla_w_o[j])
        else:
            y = _fox(h, fox_w_in[j], fox_b_f[j], fox_w_o[j])
        x = _layer_norm(DEEPNORM_ALPHA * x + (1.0 + g_a) * y, ln1_g[i], ln1_b[i])

        h = x * (1.0 + sc_f) + sh_f
        y = _swiglu(h, ffn_w1[i], ffn_w3[i], ffn_w2[i])
        x = _layer_norm(DEEPNORM_ALPHA * x + (1.0 + g_f) * y, ln2_g[i], ln2_b[i])
    return x


_drawn_inputs = setup_inputs


def setup_inputs(seed=0):
    import zlib

    import numpy as np

    out = dict(_drawn_inputs(seed))
    spreads = {}
    factors = {'ada_b': 6.627, 'mla_q_norm': 8.0, 'mla_kv_norm': 8.0, 'mla_w_uk': 2.95, 'fox_b_f': 27.312}
    for name, (base, spread) in spreads.items():
        noise = np.random.default_rng([zlib.crc32(name.encode()), seed]).standard_normal(out[name].shape)
        drawn = base * np.exp(spread * noise) if base else spread * noise
        out[name] = __import__('jax').numpy.asarray(drawn.astype(out[name].dtype))
    for name, factor in factors.items():
        out[name] = (out[name] * factor).astype(out[name].dtype)
    return out
```

```python
from contextlib import ExitStack

import numpy as np

import concourse.bass as bass
from concourse import mybir

F32 = mybir.dt.float32
F32R = mybir.dt.float32r
I32 = mybir.dt.int32
ALU = mybir.AluOpType
ACT = mybir.ActivationFunctionType

P = 128
D = 2048
S = 256
T = S // P
KC = D // P
LAYERS = 2
CHUNK = 64
H = 16
DH = 128
LORA = 512
ROPE = 64
RH = ROPE // 2
QH = DH + ROPE
ROPE_THETA = 10000.0
D_FF = -(-8 * D // (3 * 256)) * 256
ALPHA = (2 * LAYERS) ** 0.25
LN_EPS = 1e-5
RMS_EPS = 1e-6
MLA_SCALE = QH ** -0.5
FOX_SCALE = DH ** -0.5
MASKED = -1e30

NB = 512
UC = 2
UNIT = UC * NB
RING = 4
SHIFT = 4
MODS = 6
FF_PASSES = [6, 5]
assert sum(FF_PASSES) * NB == D_FF
U_CHUNKS = max(FF_PASSES) * NB // P
SH_A, SC_A, G_A, SH_F, SC_F, G_F = range(MODS)
FIRST_SLOTS = 6
EARLY = SC_F
EARLY_UNITS = range(26, 46, 4)
EARLY_LAG = 2
EARLY_REST = 48
POOL_PARTS = [G_A, SH_F, G_F] + [MODS + s for s in range(MODS)]


def early_chunks(unit):
    if unit in EARLY_UNITS:
        return [EARLY_UNITS.index(unit)]
    return range(len(EARLY_UNITS), KC) if unit == EARLY_REST else []


class Count:

    def __init__(self):
        self.n, self.i, self.per, self.start = 0, None, 0, 0

    def at(self, d=0):
        return self.n + d if self.i is None else self.i * self.per + (self.n + d)

    def enter(self, i, per):
        self.i, self.per, self.start = i, per, self.n

    def leave(self, times):
        assert self.n == self.start + self.per, (self.n, self.start, self.per)
        self.n, self.i = self.start + self.per * times, None


class Place:

    def __init__(self):
        self.unit, self.block, self.turn = Count(), Count(), Count()
        self.turn_act, self.step = Count(), Count()

    def all(self):
        return self.unit, self.block, self.turn, self.turn_act, self.step


def loop(eng, times, place, body, *, units=0, blocks=0, turns=0, turns_act=0, steps=0):
    with eng.Fori(0, times) as i:
        for count, per in zip(place.all(), (units, blocks, turns, turns_act, steps)):
            count.enter(i, per)
        body(i)
    for count in place.all():
        count.leave(times)


def two_pi_parts():
    left, parts = 2 * np.pi, []
    for _ in range(4):
        e = int(np.floor(np.log2(left)))
        piece = np.floor(left / 2.0 ** (e - 7)) * 2.0 ** (e - 7)
        parts.append(float(piece))
        left -= piece
    return parts + [float(np.float32(left))]


def trunk(nc, A, out):
    x_d = A["x"][0].rearrange("(t p) d -> p t d", p=P)
    out_d = out[0].rearrange("(t p) d -> p t d", p=P)

    def weight(w):
        return w.rearrange("(c p) n -> p c n", p=P)

    base = -(-nc.sbuf_base // 32) * 32
    at = [base]

    def place_at(name, shape, dt, offset):
        return nc.alloc_sbuf_tensor_at(name, shape, dt, offset=offset)

    def new(name, shape, dt=F32):
        here = at[0]
        at[0] += -(-int(np.prod(shape[1:])) * 4 // 32) * 32
        return place_at(name, shape, dt, here)

    KB = 1024
    a0 = at[0]
    hT_hi = new("hT_hi", [P, KC, S], F32R)
    hT_lo = new("hT_lo", [P, KC, S], F32R)
    mla_k = place_at("mla_k", [P, T, D], F32, a0)
    first_acc = place_at("first_acc", [P, 2, D], F32, a0)
    early_w = place_at("early_w", [P, 2, D], F32, a0 + 16 * KB)
    b0 = at[0]
    at[0] += 48 * KB
    first_w = place_at("first_w", [P, FIRST_SLOTS, D], F32, b0)
    mla_q = place_at("mla_q", [P, T, H * QH], F32, b0)
    mla_v = place_at("mla_v", [P, T, D], F32, b0 + 24 * KB)
    qlT_hi = place_at("qlT_hi", [P, 4, S], F32R, b0 + 24 * KB)
    qlT_lo = place_at("qlT_lo", [P, 4, S], F32R, b0 + 28 * KB)
    lat = place_at("lat", [P, 2, T, LORA], F32, b0 + 32 * KB)
    kvT_hi = place_at("kvT_hi", [P, 4, S], F32R, b0 + 40 * KB)
    kvT_lo = place_at("kvT_lo", [P, 4, S], F32R, b0 + 44 * KB)
    fox_qkv = place_at("fox_qkv", [P, T, 3 * D], F32, b0)
    uT_hi = place_at("uT_hi", [P, U_CHUNKS, S], F32R, b0)
    uT_lo = place_at("uT_lo", [P, U_CHUNKS, S], F32R, b0 + 24 * KB)
    c0 = at[0]
    ln_bc = new("ln_bc", [P, 2, D])
    qkT = place_at("qkT", [P, 2, 2 * S], F32, c0)
    qpT = place_at("qpT", [ROPE, 2, S], F32, c0 + 4 * KB)
    kpT = place_at("kpT", [ROPE, S], F32, c0 + 6 * KB)
    s_sb = place_at("s_sb", [P, 2, 3 * P], F32, c0 + 7 * KB)
    p_sb = place_at("p_sb", [P, 2, 3 * P], F32, c0 + 10 * KB)
    pT = place_at("pT", [P, 2, 3 * P], F32, c0 + 13 * KB)
    rope_t = place_at("rope_t", [P, 4, H, RH], F32, c0 + 8 * KB)
    rows = place_at("rows", [P, 4, P], F32, c0)
    ang = place_at("ang", [P, 6, T, RH], F32, c0 + 2 * KB)
    silu = place_at("silu", [P, T, NB], F32, c0)
    u = place_at("u", [P, T, NB], F32, c0 + 4 * KB)

    xa = new("xa", [P, T, D])
    gate = new("gate", [P, D])
    ada_acc = new("ada_acc", [P, D])
    ada_w = new("ada_w", [P, 2, D])
    raw = new("raw", [P, RING, UNIT])
    whi = new("whi", [P, RING, UNIT], F32R)
    wlo = new("wlo", [P, RING, UNIT], F32R)
    tmp = new("tmp", [P, 2, NB])
    ident = new("ident", [P, P])
    tri = new("tri", [P, S])
    mla_mask = new("mla_mask", [P, 3 * P])
    fox_mask = new("fox_mask", [P, 3 * P])
    ones = new("ones", [P, 8])
    ln_col = new("ln_col", [P, 4, LAYERS, KC])
    nrm_col = new("nrm_col", [P, 24])
    adab_col = new("adab_col", [P, LAYERS * MODS, KC])
    c_act = new("c_act", [P, KC])
    mod = new("mod", [P, LAYERS * MODS, KC])
    gcol = new("gcol", [P, 2, KC])
    stats = new("stats", [P, T, 4 * 6])
    mv = new("mv", [P, T, 2])
    ssq = new("ssq", [P, 2, T])
    var = new("var", [P, 2])
    root = new("root", [P, 2])
    rstd = new("rstd", [P, 2])
    nt = new("nt", [P, 2])
    nmean = new("nmean", [P, 2])
    cos = new("cos", [P, T, RH])
    sin = new("sin", [P, T, RH])
    inv = new("inv", [P, RH])
    pos_i = new("pos_i", [P, T], I32)
    pos_f = new("pos_f", [P, T])
    kpe = new("kpe", [P, T, ROPE])
    bf = new("bf", [P, H])
    logf = new("logf", [P, 8, T, H])
    cumT = new("cumT", [H, 2, S])
    smax = new("smax", [P, 2, 2])
    nmax = new("nmax", [P, 2, 2])
    psums = new("psums", [P, 2, 2])
    pinv = new("pinv", [P, 2, 2])
    assert at[0] <= nc.sbuf_usable_end, (at[0], nc.sbuf_usable_end)

    with ExitStack() as ctx:
        ps = ctx.enter_context(nc.psum_tensor("ps", [P, 8, NB], F32))

        def sem(name):
            return ctx.enter_context(nc.semaphore(name))

        small_in = sem("small_in")
        x_in = sem("x_in")
        first_in = [sem(f"first_in{i}") for i in range(FIRST_SLOTS)]
        early_in = [sem(f"early_in{i}") for i in range(2)]
        raw_in = [sem(f"raw_in{i}") for i in range(RING)]
        ada_in = [sem(f"ada_in{i}") for i in range(2)]
        ln_in = sem("ln_in")
        out_done = sem("out_done")
        consts = sem("consts")
        hi_ready = sem("hi_ready")
        lo_ready = sem("lo_ready")
        units_used = sem("units_used")
        pair_read = [sem(f"pair_read{i}") for i in range(2)]
        turned = sem("turned")
        turned_act = sem("turned_act")
        turned_out = sem("turned_out")
        dve_step = sem("dve_step")
        act_step = sem("act_step")
        pool_mac = sem("pool_mac")
        pool_prod = sem("pool_prod")
        chunk_seen = sem("chunk_seen")
        first_mac = sem("first_mac")
        early_mac = sem("early_mac")
        acc_reduced = sem("acc_reduced")
        c_ready = sem("c_ready")
        angles = sem("angles")
        sincos = sem("sincos")
        ssq_ready = sem("ssq_ready")
        root_ready = sem("root_ready")
        rstd_ready = sem("rstd_ready")
        lat_ready = sem("lat_ready")
        var_ready = sem("var_ready")
        norm_ready = sem("norm_ready")
        xa_updated = sem("xa_updated")
        q_roped = sem("q_roped")
        logf_ready = sem("logf_ready")
        logf_in = sem("logf_in")
        expf = sem("expf")
        qk_turned = sem("qk_turned")
        qk_copied = sem("qk_copied")
        qp_turned = sem("qp_turned")
        qp_copied = sem("qp_copied")
        scored = sem("scored")
        masked = sem("masked")
        max_ready = sem("max_ready")
        exp_done = sem("exp_done")
        p_turned = sem("p_turned")
        pT_copied = sem("pT_copied")
        pv_done = sem("pv_done")
        o_scaled = sem("o_scaled")
        out_ready = sem("out_ready")

        block = ctx.enter_context(nc.Block())

        n_small = 13
        n_consts = 5 + 2 + 4

        def flat(tile):
            return tile[:, :, :].rearrange("p c s -> p (c s)")

        def part_in_down(l, n):
            return l == 0 or n == 0

        def pair_uses(b, p):
            n = (b.n + 1 - p) // 2
            return n if b.i is None else b.i * (b.per // 2) + n

        def unit_loads(unit):
            n = 16 * (unit.n // RING + 1)
            return n if unit.i is None else unit.i * (16 * unit.per // RING) + n

        @block.sync
        def _(sp):
            pl = Place()

            def small(dst, src):
                sp.dma_start(dst, src).then_inc(small_in, 16)

            for r, name in enumerate(("ln1_g", "ln1_b", "ln2_g", "ln2_b")):
                small(rows[r * 32:(r + 1) * 32, 0, :], A[name].rearrange("l (c p) -> (l c) p", p=P))
            small(rows[0:KC, 1, :], A["c"].rearrange("b (c p) -> (b c) p", p=P))
            small(rows[KC:KC + 4, 1, :], A["mla_q_norm"].rearrange("b (c p) -> (b c) p", p=P))
            small(rows[KC + 4:KC + 8, 1, :], A["mla_kv_norm"].rearrange("b (c p) -> (b c) p", p=P))
            for l in range(LAYERS):
                small(rows[0:MODS * KC, 2 + l, :], A["ada_b"][l].rearrange("(c p) -> c p", p=P))
            for t in range(T):
                small(pos_i[:, t:t + 1],
                      A["positions"][0, t * P:(t + 1) * P].rearrange("(p a) -> p a", a=1))
            small(inv[:, :], A["inv_freq"].partition_broadcast(P))
            small(bf[:, :], A["fox_b_f"][0].partition_broadcast(P))

            for n in range(2 * KC):
                k, part, slot = n // 2, (SH_A, SC_A)[n % 2], n % FIRST_SLOTS
                if n >= FIRST_SLOTS:
                    sp.wait_ge(first_mac, n - FIRST_SLOTS + 1)
                sp.dma_start(first_w[:, slot, :],
                             A["ada_w"][0, k * P:(k + 1) * P, part * D:(part + 1) * D]
                             ).then_inc(first_in[slot], 16)
                if n == FIRST_SLOTS - 1:
                    sp.dma_start(xa[:, :, :], x_d).then_inc(x_in, 16)

            def load(w, chunk, col, chunks=UC, width=NB):
                s = pl.unit.n % RING
                if pl.unit.i is not None or pl.unit.n >= RING:
                    sp.wait_ge(lo_ready, pl.unit.at(1 - RING))
                dst = raw[:, s, 0:chunks * width].rearrange("p (c n) -> p c n", c=chunks)
                sp.dma_start(dst, w[:, chunk:chunk + chunks, bass.ds(col, width)]
                             ).then_inc(raw_in[s], 16)
                if pl.unit.i is None:
                    for m in early_chunks(pl.unit.n):
                        load_early(m)
                pl.unit.n += 1

            def load_early(m):
                if m < 2:
                    sp.wait_ge(units_used, 2 * KC // UC + 1)
                else:
                    sp.wait_ge(early_mac, m - 1)
                sp.dma_start(early_w[:, m % 2, :],
                             A["ada_w"][0, m * P:(m + 1) * P, EARLY * D:(EARLY + 1) * D]
                             ).then_inc(early_in[m % 2], 16)

            def load_block(w, col, chunk0, chunks):
                for c in range(0, chunks, UC):
                    load(w, chunk0 + c, col)

            def load_ln(k, names, layer):
                if k % 2 == 0:
                    sp.wait_ge(o_scaled, H * (layer + 1))
                else:
                    sp.wait_ge(units_used, pl.unit.at(SHIFT - 4 * (FF_PASSES[-1] * NB // P) // UC))
                for j, name in enumerate(names):
                    sp.dma_start(ln_bc[:, j, :], A[name][layer].partition_broadcast(P)
                                 ).then_inc(ln_in, 16)

            def load_wo(w):
                loop(sp, 2, pl, lambda i: [load_block(w, i * (2 * NB) + j * NB, 0, KC)
                                           for j in range(2)], units=2 * KC // UC)

            def load_ffn(l):
                w1, w3, w2 = (weight(A[n][l]) for n in ("ffn_w1", "ffn_w3", "ffn_w2"))
                first = 0
                for nb in FF_PASSES:
                    def up(i):
                        load_block(w1, i * NB + first * NB, 0, KC)
                        load_block(w3, i * NB + first * NB, 0, KC)
                    loop(sp, nb, pl, up, units=2 * KC // UC)
                    loop(sp, 2, pl, lambda i: [load_block(w2, i * (2 * NB) + j * NB, 4 * first, 4 * nb)
                                               for j in range(2)], units=2 * 4 * nb // UC)
                    first += nb

            down = weight(A["mla_w_down"][0])
            load_block(down, 0, 0, KC)
            load_block(down, LORA, 0, KC)
            load(down, 0, 2 * LORA, chunks=KC, width=ROPE)
            for name, cols in (("mla_w_uq", H * QH), ("mla_w_uk", D), ("mla_w_uv", D)):
                for col in range(0, cols, NB):
                    load_block(weight(A[name][0]), col, 0, LORA // P)
            for col in range(0, D, NB):
                load_block(weight(A["mla_w_o"][0]), col, 0, KC)
            load_ln(0, ("ln1_g", "ln1_b"), 0)
            load_ffn(0)
            load_ln(1, ("ln2_g", "ln2_b"), 0)
            w_in = weight(A["fox_w_in"][0])
            loop(sp, 6, pl, lambda i: [load_block(w_in, i * (2 * NB) + j * NB, 0, KC)
                                       for j in range(2)], units=2 * KC // UC)
            load(w_in, 0, 3 * D, chunks=KC, width=H)
            load_wo(weight(A["fox_w_o"][0]))
            load_ln(2, ("ln1_g", "ln1_b"), 1)
            load_ffn(1)
            load_ln(3, ("ln2_g", "ln2_b"), 1)
            for t in range(T):
                sp.wait_ge(out_ready, t + 1)
                sp.dma_start(out_d[:, t, :], xa[:, t, :]).then_inc(out_done, 16)
            sp.wait_ge(out_done, 16 * T)

        @block.gpsimd
        def _(pool):
            nc.gpsimd.memset(ones[:, :], 1.0).then_inc(consts, 1)
            nc.gpsimd.memset(ident[:, :], 0.0).then_inc(consts, 1)
            nc.gpsimd.memset(tri[:, :], 1.0).then_inc(consts, 1)
            nc.gpsimd.memset(mla_mask[:, :], 0.0).then_inc(consts, 1)
            nc.gpsimd.memset(fox_mask[:, :], 0.0).then_inc(consts, 1)
            pool.wait_ge(consts, 5)
            nc.gpsimd.affine_select(out=ident[:, :], in_=ident[:, :], compare_op=ALU.not_equal,
                                    fill=1.0, base=0, pattern=[[-1, P]],
                                    channel_multiplier=1).then_inc(consts, 1)
            nc.gpsimd.affine_select(out=tri[:, 0:P], in_=tri[:, 0:P], compare_op=ALU.is_ge,
                                    fill=0.0, base=0, pattern=[[1, P]],
                                    channel_multiplier=-1).then_inc(consts, 1)
            for o in (0, 2 * P):
                nc.gpsimd.memset(mla_mask[0:CHUNK, o + CHUNK:o + P], MASKED).then_inc(consts, 1)
                nc.gpsimd.affine_select(out=fox_mask[:, o:o + P], in_=fox_mask[:, o:o + P],
                                        compare_op=ALU.is_ge, fill=MASKED, base=0,
                                        pattern=[[-1, P]], channel_multiplier=1).then_inc(consts, 1)

            def part(layer, s, r):
                for k in range(KC + 1):
                    if k < KC:
                        if k >= 2 or not isinstance(r, int) or r > 0:
                            pool.wait_ge(pool_mac, r * KC + (k - 1))
                        pool.dma_start(ada_w[:, k % 2, :],
                                       A["ada_w"][layer, k * P:(k + 1) * P, bass.ds(s * D, D)]
                                       ).then_inc(ada_in[k % 2], 16)
                    if k == 0:
                        continue
                    j = k - 1
                    w = ada_w[:, j % 2, :]
                    pool.wait_ge(ada_in[j % 2], r * (8 * KC) + 16 * (j // 2 + 1))
                    pool.sem_inc(chunk_seen, 1)
                    if j == 0:
                        nc.gpsimd.tensor_scalar(ada_acc[:, :], w, c_act[:, 0:1], 0.0,
                                                ALU.mult, ALU.add).then_inc(pool_mac, 1)
                        continue
                    nc.gpsimd.tensor_scalar(w, w, c_act[:, j:j + 1], 0.0,
                                            ALU.mult, ALU.add).then_inc(pool_prod, 1)
                    pool.wait_ge(pool_prod, r * (KC - 1) + j)
                    pool.wait_ge(pool_mac, r * KC + j)
                    nc.gpsimd.tensor_tensor(ada_acc[:, :], ada_acc[:, :], w, ALU.add
                                            ).then_inc(pool_mac, 1)

            pool.wait_ge(first_mac, 2 * KC - 4)
            part(0, G_A, 0)
            pool.wait_ge(acc_reduced, 3)
            part(0, SH_F, 1)
            pool.wait_ge(acc_reduced, MODS - 1)
            part(0, G_F, 2)
            with pool.Fori(0, MODS) as s:
                pool.wait_ge(acc_reduced, s + MODS)
                part(1, s, s + 3)

        @block.scalar
        def _(act):
            pl = Place()

            def split(n):
                for _ in range(n):
                    s = pl.unit.n % RING
                    act.wait_ge(raw_in[s], unit_loads(pl.unit))
                    if pl.unit.i is not None or pl.unit.n >= RING:
                        act.wait_ge(units_used, pl.unit.at(1 - RING))
                    nc.scalar.activation(whi[:, s, :], raw[:, s, :], ACT.Copy).then_inc(hi_ready, 1)
                    pl.unit.n += 1

            def block_done():
                act.wait_ge(units_used, pl.unit.at(-SHIFT))

            def free_pair(ins):
                ins.then_inc(pair_read[pl.block.n % 2], 1)
                pl.block.n += 1

            def copy_block(dst, width=NB):
                block_done()
                p = 2 * (pl.block.n % 2)
                for t in range(T):
                    ins = nc.scalar.activation(dst(t), ps[:, p + t, 0:width], ACT.Copy)
                free_pair(ins)

            def turn_affine(banks, gain, offset=None):
                for b in range(banks):
                    act.wait_ge(turned, pl.turn.at(1))
                    act.wait_ge(turned_out, pl.turn.at(-1))
                    for c in range(UC):
                        i, o = (x[:, c * S:(c + 1) * S] for x in (ps[:, 4 + pl.turn.n % 2, :],
                                                                  tmp[:, pl.turn.n % 2, :]))
                        if offset is None:
                            ins = nc.scalar.activation(o, i, ACT.Copy, scale=gain(UC * b + c))
                        else:
                            ins = nc.scalar.activation(o, i, ACT.Identity, scale=gain(UC * b + c),
                                                       bias=offset(UC * b + c))
                    ins.then_inc(turned_act, 1)
                    pl.turn.n += 1
                    pl.turn_act.n += 1

            def turn_plain(dst, chunk, banks):
                for b in range(banks):
                    act.wait_ge(turned, pl.turn.at(1))
                    nc.scalar.activation(flat(dst)[:, bass.ds(chunk * S + UC * b * S, UC * S)],
                                         ps[:, 4 + pl.turn.n % 2, :], ACT.Copy
                                         ).then_inc(turned_act, 1)
                    pl.turn.n += 1
                    pl.turn_act.n += 1

            def h_turns():
                turn_affine(KC // UC, lambda c: gcol[:, 0, c:c + 1], lambda c: gcol[:, 1, c:c + 1])

            def take_root(norm):
                act.wait_ge(var_ready, norm + 1)
                nc.scalar.activation(root[:, :], var[:, :], ACT.Sqrt).then_inc(root_ready, 1)

            def latent(which):
                block_done()
                act.wait_ge(turned_out, pl.turn.at())
                p = 2 * (pl.block.n % 2)
                for t in range(T):
                    ins = nc.scalar.activation(tmp[:, t, :], ps[:, p + t, :], ACT.Square,
                                               accum_out=ssq[:, which, t:t + 1])
                ins.then_inc(ssq_ready, 1)
                take_root(which)
                act.wait_ge(rstd_ready, which + 1)
                for t in range(T):
                    ins = nc.scalar.activation(lat[:, which, t, :], ps[:, p + t, :], ACT.Copy,
                                               scale=rstd[:, t:t + 1])
                free_pair(ins)

            def attention(layer, scale, out_tile):
                g0 = H * layer
                for i in range(H + 3):
                    if i < H:
                        g = g0 + i
                        act.wait_ge(qk_turned, g + 1)
                        if g >= 2:
                            act.wait_ge(scored, g - 1)
                        nc.scalar.activation(qkT[:, g % 2, :], ps[:, g % 2, :], ACT.Copy
                                             ).then_inc(qk_copied, 1)
                    if 1 <= i <= H:
                        g = g0 + i - 1
                        act.wait_ge(max_ready, g + 1)
                        if g >= 2:
                            act.wait_ge(pT_copied, g - 1)
                        for t, a, b in ((0, 0, P), (1, P, 3 * P)):
                            ins = nc.scalar.activation(p_sb[:, g % 2, a:b], s_sb[:, g % 2, a:b],
                                                       ACT.Exp, bias=nmax[:, g % 2, t:t + 1],
                                                       scale=scale,
                                                       accum_out=psums[:, g % 2, t:t + 1])
                        ins.then_inc(exp_done, 1)
                    if i >= 3:
                        g = g0 + i - 3
                        act.wait_ge(pv_done, g + 1)
                        for t in range(T):
                            ins = nc.scalar.activation(out_tile(t, i - 3),
                                                       ps[:, 6 + g % 2, t * P:(t + 1) * P],
                                                       ACT.Copy, scale=pinv[:, g % 2, t:t + 1])
                        ins.then_inc(o_scaled, 1)

            def w_o(layer):
                pl.turn.n += (1 - layer) + 4
                turn_plain(hT_hi, 0, KC // UC)

                def body(i):
                    split(2 * KC // UC)
                    pl.block.n += 2
                loop(act, 2, pl, body, units=2 * KC // UC, blocks=2)
                pl.turn.n += 1

            def ffn(l):
                for n, nb in enumerate(FF_PASSES):
                    def up(i, first=False):
                        split(KC // UC)
                        block_done()
                        pair = pl.block.n % 2
                        if first and n == 0:
                            act.wait_ge(xa_updated, 2 * l + 1)
                        act.wait_ge(pair_read[1 - pair], pair_uses(pl.block, 1 - pair))
                        for t in range(T):
                            ins = nc.scalar.activation(silu[:, t, :], ps[:, 2 * pair + t, :],
                                                       ACT.Silu)
                        free_pair(ins)
                        if not first:
                            turn_plain(uT_hi, i * 4, 2)
                        split(KC // UC)
                        pl.block.n += 1
                    if n == 0:
                        h_turns()
                    up(0, first=True)
                    loop(act, nb - 1, pl, up, units=2 * KC // UC, blocks=2, turns=2, turns_act=2)
                    with_part, with_gate = part_in_down(l, n), n == 0
                    pl.turn.n += with_part
                    turn_plain(uT_hi, 4 * (nb - 1), 2)
                    pl.turn.n += 4 * with_gate
                    end = l == LAYERS - 1 and n == len(FF_PASSES) - 1
                    split(4 * 4 * nb // UC - SHIFT * end)
                    pl.block.n += 4
                    if l == 0 and n == 0:
                        pl.turn.n += 1

            act.wait_ge(turned_out, 1)
            nc.scalar.activation(c_act[:, :], nrm_col[:, 0:KC], ACT.Silu).then_inc(c_ready, 1)
            act.wait_ge(angles, 1)
            nc.scalar.activation(sin[:, :, :], ang[:, 4, :, :], ACT.Sin)
            nc.scalar.activation(cos[:, :, :], ang[:, 5, :, :], ACT.Sin).then_inc(sincos, 1)
            pl.turn.n += 3
            split(SHIFT)

            h_turns()
            split(KC // UC)
            latent(0)
            split(KC // UC)
            turn_affine(2, lambda c: nrm_col[:, KC + c:KC + c + 1])
            latent(1)
            split(1)
            copy_block(lambda t: kpe[:, t, :], width=ROPE)
            for j in range(H * QH // NB):
                split(LORA // P // UC)
                copy_block(lambda t: mla_q[:, t, j * NB:(j + 1) * NB])
                if j == 0:
                    turn_affine(2, lambda c: nrm_col[:, KC + 4 + c:KC + 5 + c])
            for dst in (mla_k, mla_v):
                for j in range(D // NB):
                    split(LORA // P // UC)
                    copy_block(lambda t: dst[:, t, j * NB:(j + 1) * NB])
            pl.turn.n += 2
            attention(0, MLA_SCALE, lambda t, h: mla_v[:, t, h * DH:(h + 1) * DH])
            w_o(0)
            take_root(2)
            ffn(0)
            take_root(3)

            h_turns()

            def qkv(i, lead=0):
                for j in range(2):
                    split(KC // UC)
                    copy_block(lambda t: fox_qkv[:, t, bass.ds(i * (2 * NB) + (lead + j) * NB, NB)])
            qkv(0)
            pl.turn.n += 1
            loop(act, 5, pl, lambda i: qkv(i, 2), units=2 * KC // UC, blocks=2)
            split(1)
            pl.block.n += 1
            act.wait_ge(logf_in, 1)
            nc.scalar.activation(logf[:, 1, :, :], logf[:, 0, :, :], ACT.Exp, scale=-1.0
                                 ).then_inc(expf, 1)
            pl.turn.n += 2
            attention(1, FOX_SCALE, lambda t, h: fox_qkv[:, t, 2 * D + h * DH:2 * D + (h + 1) * DH])
            w_o(1)
            take_root(4)
            ffn(1)
            take_root(5)

        @block.vector
        def _(dve):
            pl = Place()

            def mark(ins):
                ins.then_inc(dve_step, 1)
                pl.step.n += 1

            def own():
                dve.wait_ge(dve_step, pl.step.at())

            def chain(ins):
                mark(ins)
                own()

            def split(n):
                for _ in range(n):
                    s = pl.unit.n % RING
                    dve.wait_ge(hi_ready, pl.unit.at(1))
                    nc.vector.tensor_tensor(wlo[:, s, :], raw[:, s, :], whi[:, s, :].bitcast(F32),
                                            ALU.subtract).then_inc(lo_ready, 1)
                    if pl.unit.i is None:
                        for m in early_chunks(pl.unit.n - EARLY_LAG):
                            early_part(m)
                    pl.unit.n += 1

            def early_part(m):
                dve.wait_ge(early_in[m % 2], 16 * (m // 2 + 1))
                if m == 0:
                    ins = nc.vector.tensor_scalar(gate[:, :], early_w[:, 0, :], c_act[:, 0:1],
                                                  None, ALU.mult)
                else:
                    dve.wait_ge(early_mac, m)
                    ins = nc.vector.scalar_tensor_tensor(out=gate[:, :], in0=early_w[:, m % 2, :],
                                                         scalar=c_act[:, m:m + 1], in1=gate[:, :],
                                                         op0=ALU.mult, op1=ALU.add)
                ins.then_inc(early_mac, 1)

            def block_done():
                dve.wait_ge(units_used, pl.unit.at(-SHIFT))

            def turn_affine(hi, lo, banks):
                for b in range(banks):
                    dve.wait_ge(turned_act, pl.turn_act.at(1))
                    o = slice(b * UC * S, (b + 1) * UC * S)
                    src = tmp[:, pl.turn.n % 2, :]
                    chain(nc.vector.tensor_copy(flat(hi)[:, o], src))
                    nc.vector.tensor_tensor(flat(lo)[:, o], src, flat(hi)[:, o].bitcast(F32),
                                            ALU.subtract).then_inc(turned_out, 1)
                    pl.turn.n += 1
                    pl.turn_act.n += 1

            def turn_plain(hi, lo, chunk, banks):
                for b in range(banks):
                    dve.wait_ge(turned_act, pl.turn_act.at(1))
                    o = bass.ds(chunk * S + UC * b * S, UC * S)
                    nc.vector.tensor_tensor(flat(lo)[:, o], ps[:, 4 + pl.turn.n % 2, :],
                                            flat(hi)[:, o].bitcast(F32), ALU.subtract
                                            ).then_inc(turned_out, 1)
                    pl.turn.n += 1
                    pl.turn_act.n += 1

            def turn_copy(dst, src):
                dve.wait_ge(turned, pl.turn.at(1))
                nc.vector.tensor_copy(dst, src(ps[:, 4 + pl.turn.n % 2, :])).then_inc(turned_out, 1)
                pl.turn.n += 1

            def turns_written():
                dve.wait_ge(turned_out, pl.turn.at())

            def ada_part(q):
                dve.wait_ge(turned, pl.turn.at(1))
                plus = 1.0 if q % MODS in (SC_A, G_A, SC_F, G_F) else 0.0
                for half, done in ((slice(0, KC // 2), acc_reduced), (slice(KC // 2, KC), turned_out)):
                    nc.vector.scalar_tensor_tensor(out=mod[:, q, half],
                                                   in0=ps[:, 4 + pl.turn.n % 2, half], scalar=plus,
                                                   in1=adab_col[:, q, half], op0=ALU.add,
                                                   op1=ALU.add).then_inc(done, 1)
                pl.turn.n += 1
                turns_written()

            def gate_in():
                for j in range(4):
                    turn_copy(gate[:, j * NB:(j + 1) * NB], lambda b: b)
                turns_written()

            def newton(norm):
                dve.wait_ge(root_ready, norm + 1)
                chain(nc.vector.reciprocal(rstd[:, :], root[:, :]))
                chain(nc.vector.tensor_tensor(nt[:, :], rstd[:, :], rstd[:, :], ALU.mult))
                chain(nc.vector.tensor_tensor(nt[:, :], nt[:, :], var[:, :], ALU.mult))
                chain(nc.vector.tensor_scalar(nt[:, :], nt[:, :], -0.5, 1.5, ALU.mult, ALU.add))
                return nc.vector.tensor_tensor(rstd[:, :], rstd[:, :], nt[:, :], ALU.mult)

            def latent(which):
                dve.wait_ge(ssq_ready, which + 1)
                nc.vector.tensor_scalar(var[:, :], ssq[:, which, :], 1.0 / LORA, RMS_EPS,
                                        ALU.mult, ALU.add).then_inc(var_ready, 1)
                newton(which).then_inc(rstd_ready, 1)
                pl.block.n += 1

            def residual(col, stat_col, last):
                block_done()
                pair = pl.block.n % 2
                own()
                for t in range(T):
                    ins = nc.vector.tensor_tensor(tmp[:, t, :], ps[:, 2 * pair + t, :],
                                                  gate[:, bass.ds(col, NB)], ALU.mult)
                ins.then_inc(pair_read[pair], 1)
                pl.block.n += 1
                dve.wait_ge(pair_read[pair], pair_uses(pl.block, pair))
                for t in range(T):
                    mark(nc.vector.tensor_tensor(xa[:, t, bass.ds(col, NB)],
                                                 xa[:, t, bass.ds(col, NB)], tmp[:, t, :],
                                                 ALU.add))
                if last:
                    own()
                    for t in range(T):
                        mark(nc.vector.bn_stats(stats[:, t, bass.ds(stat_col, 6)],
                                                xa[:, t, bass.ds(col, NB)]))

            def affine_cols(cols, layer, to_layer, sh, sc):
                q = to_layer * MODS
                chain(nc.vector.tensor_tensor(gcol[:, 0, :], ln_col[:, cols, layer, :],
                                              mod[:, q + sc, :], ALU.mult))
                chain(nc.vector.tensor_tensor(gcol[:, 1, :], ln_col[:, cols + 1, layer, :],
                                              mod[:, q + sc, :], ALU.mult))
                chain(nc.vector.tensor_tensor(gcol[:, 1, :], gcol[:, 1, :], mod[:, q + sh, :],
                                              ALU.add))

            def layer_norm(k, cols=None):
                own()
                for t in range(T):
                    mark(nc.vector.bn_aggr(mv[:, t, :], stats[:, t, :]))
                own()
                nc.vector.tensor_scalar(var[:, :], mv[:, :, 1], LN_EPS, None, ALU.add
                                        ).then_inc(var_ready, 1)
                if cols is not None:
                    affine_cols(*cols)
                chain(newton(2 + k))
                chain(nc.vector.scalar_tensor_tensor(out=nmean[:, :], in0=mv[:, :, 0], scalar=-1.0,
                                                     in1=rstd[:, :], op0=ALU.mult, op1=ALU.mult))
                for t in range(T):
                    ins = nc.vector.tensor_scalar(xa[:, t, :], xa[:, t, :], rstd[:, t:t + 1],
                                                  nmean[:, t:t + 1], ALU.mult, ALU.add)
                ins.then_inc(norm_ready, 1)
                dve.wait_ge(norm_ready, k + 2)

            def scale_xa(t, k, alpha=ALPHA):
                if k is None:
                    mark(nc.vector.tensor_scalar(xa[:, t, :], xa[:, t, :], alpha, None, ALU.mult))
                    return
                dve.wait_ge(ln_in, 32 * (k + 1))
                chain(nc.vector.scalar_tensor_tensor(out=xa[:, t, :], in0=xa[:, t, :], scalar=alpha,
                                                     in1=ln_bc[:, 0, :], op0=ALU.mult,
                                                     op1=ALU.mult))
                ins = nc.vector.scalar_tensor_tensor(out=xa[:, t, :], in0=ln_bc[:, 1, :],
                                                     scalar=alpha, in1=xa[:, t, :], op0=ALU.mult,
                                                     op1=ALU.add)
                if alpha == 1.0:
                    ins.then_inc(out_ready, 1)
                    return
                if t == T - 1:
                    ins.then_inc(xa_updated, 1)
                    dve.wait_ge(xa_updated, k + 1)
                else:
                    mark(ins)

            def split_scaling(k):
                for t in range(T):
                    split(KC // UC // T)
                    scale_xa(t, k)

            def rope(x0, x1, cs, sn, t0, t1, t2, t3):
                mark(nc.vector.tensor_tensor(t0, x0, cs, ALU.mult))
                mark(nc.vector.tensor_tensor(t1, x1, sn, ALU.mult))
                mark(nc.vector.tensor_tensor(t2, x0, sn, ALU.mult))
                mark(nc.vector.tensor_tensor(t3, x1, cs, ALU.mult))
                own()
                mark(nc.vector.tensor_tensor(x0, t0, t1, ALU.subtract))
                return nc.vector.tensor_tensor(x1, t2, t3, ALU.add)

            def attention(layer, scale, mask, rotary):
                g0 = H * layer
                for i in range(H + 2):
                    if 1 <= i <= H:
                        g = g0 + i - 1
                        dve.wait_ge(scored, g + 1)
                        if g >= 2:
                            dve.wait_ge(exp_done, g - 1)
                        for t, a, b in ((0, 0, P), (1, P, 3 * P)):
                            ins = nc.vector.tensor_tensor_reduce(
                                s_sb[:, g % 2, a:b], ps[:, 2 + g % 2, a:b], mask[:, a:b], 1.0,
                                -3.0e38, ALU.add, ALU.max, smax[:, g % 2, t:t + 1])
                        ins.then_inc(masked, 1)
                        dve.wait_ge(masked, g + 1)
                        nc.vector.tensor_scalar(nmax[:, g % 2, :], smax[:, g % 2, :], -scale, None,
                                                ALU.mult).then_inc(max_ready, 1)
                    if rotary and i < H:
                        g = g0 + i
                        dve.wait_ge(qp_turned, g + 1)
                        if g >= 2:
                            dve.wait_ge(scored, g - 1)
                        nc.vector.tensor_copy(qpT[:, g % 2, :], ps[0:ROPE, 6 + g % 2, S:2 * S]
                                              ).then_inc(qp_copied, 1)
                    if i >= 2:
                        g = g0 + i - 2
                        dve.wait_ge(p_turned, g + 1)
                        if g >= 2:
                            dve.wait_ge(o_scaled, g - 1)
                        nc.vector.reciprocal(pinv[:, g % 2, :], psums[:, g % 2, :])
                        nc.vector.tensor_copy(pT[:, g % 2, :], ps[:, 4 + g % 2, 0:3 * P]
                                              ).then_inc(pT_copied, 1)
                    if layer == 0 and i >= 1 and len(EARLY_UNITS) + i - 1 < KC:
                        early_part(len(EARLY_UNITS) + i - 1)

            def w_o(layer):
                if layer == 0:
                    ada_part(EARLY)
                gate_in()
                turn_plain(hT_hi, hT_lo, 0, KC // UC)

                def body(i):
                    for j in range(2):
                        split(KC // UC)
                        residual(i * (2 * NB) + j * NB, i * 12 + j * 6, True)
                loop(dve, 2, pl, body, units=2 * KC // UC, blocks=2, steps=8)
                ada_part((SH_F, 10)[layer])

            def ffn(l):
                for n, nb in enumerate(FF_PASSES):
                    last = n == len(FF_PASSES) - 1

                    def up(i, first=False):
                        if first and n == 0:
                            split_scaling(2 * l)
                        else:
                            split(KC // UC)
                        if not first:
                            turn_plain(uT_hi, uT_lo, i * 4, 2)
                        split(KC // UC)
                        pl.block.n += 1
                        block_done()
                        pair = pl.block.n % 2
                        dve.wait_ge(pair_read[1 - pair], pair_uses(pl.block, 1 - pair))
                        for t in range(T):
                            ins = nc.vector.tensor_tensor(u[:, t, :], silu[:, t, :],
                                                          ps[:, 2 * pair + t, :], ALU.mult)
                        ins.then_inc(pair_read[pair], 1)
                        pl.block.n += 1
                    if n == 0:
                        turn_affine(hT_hi, hT_lo, KC // UC)
                    up(0, first=True)
                    loop(dve, nb - 1, pl, up, units=2 * KC // UC, blocks=2, turns=2, turns_act=2)
                    if part_in_down(l, n):
                        ada_part(l * MODS + G_F if n == 0 else 7)
                    turn_plain(uT_hi, uT_lo, 4 * (nb - 1), 2)
                    if n == 0:
                        gate_in()
                    nu = 4 * nb // UC
                    for j in range(4):
                        end = last and l == LAYERS - 1 and j == 3
                        split(nu - SHIFT * end)
                        pl.unit.n += SHIFT * end
                        residual(j * NB, j * 6, last)
                    if l == 0 and n == 0:
                        ada_part(6)

            dve.wait_ge(turned, 1)
            nc.vector.tensor_copy(ln_col[:, :, :, :].rearrange("p a l c -> p (a l c)"),
                                  ps[:, 4, 0:P])
            nc.vector.tensor_copy(adab_col[:, :, :].rearrange("p q c -> p (q c)"),
                                  ps[:, 4, P + 24:P + 24 + LAYERS * MODS * KC])
            nc.vector.tensor_copy(nrm_col[:, :], ps[:, 4, P:P + 24]).then_inc(turned_out, 1)
            pl.turn.n += 1

            dve.wait_ge(small_in, 16 * n_small)
            chain(nc.vector.tensor_copy(pos_f[:, :], pos_i[:, :]))
            for t in range(T):
                mark(nc.vector.tensor_scalar(ang[:, 0, t, :], inv[:, :], pos_f[:, t:t + 1], None,
                                             ALU.mult))
            own()
            whole = 1.5 * 2.0 ** 23
            chain(nc.vector.tensor_scalar(ang[:, 1, :, :], ang[:, 0, :, :],
                                          float(1 / (2 * np.pi)), None, ALU.mult))
            chain(nc.vector.tensor_scalar(ang[:, 1, :, :], ang[:, 1, :, :], whole, None, ALU.add))
            chain(nc.vector.tensor_scalar(ang[:, 1, :, :], ang[:, 1, :, :], -whole, None, ALU.add))
            for piece in two_pi_parts():
                chain(nc.vector.scalar_tensor_tensor(out=ang[:, 0, :, :], in0=ang[:, 1, :, :],
                                                     scalar=-piece, in1=ang[:, 0, :, :],
                                                     op0=ALU.mult, op1=ALU.add))
            chain(nc.vector.tensor_scalar(ang[:, 4, :, :], ang[:, 0, :, :], 3.1415925, -3.1415925,
                                          ALU.min, ALU.max))
            chain(nc.vector.tensor_scalar(ang[:, 2, :, :], ang[:, 4, :, :], -1.0, None, ALU.mult))
            chain(nc.vector.tensor_tensor(ang[:, 3, :, :], ang[:, 4, :, :], ang[:, 2, :, :],
                                          ALU.max))
            nc.vector.tensor_scalar(ang[:, 5, :, :], ang[:, 3, :, :], -1.0, float(np.pi / 2),
                                    ALU.mult, ALU.add).then_inc(angles, 1)

            dve.wait_ge(c_ready, 1)
            for n in range(2 * KC):
                k, acc, slot = n // 2, first_acc[:, n % 2, :], n % FIRST_SLOTS
                dve.wait_ge(first_in[slot], 16 * (n // FIRST_SLOTS + 1))
                if k == 0:
                    ins = nc.vector.tensor_scalar(acc, first_w[:, slot, :], c_act[:, 0:1],
                                                  None, ALU.mult)
                else:
                    dve.wait_ge(first_mac, n - 1)
                    ins = nc.vector.scalar_tensor_tensor(out=acc, in0=first_w[:, slot, :],
                                                         scalar=c_act[:, k:k + 1], in1=acc,
                                                         op0=ALU.mult, op1=ALU.add)
                ins.then_inc(first_mac, 1)
            split(SHIFT)
            ada_part(SH_A)
            ada_part(SC_A)
            nc.vector.tensor_copy(gcol[:, 0, :], mod[:, SC_A, :])
            nc.vector.tensor_copy(gcol[:, 1, :], mod[:, SH_A, :]).then_inc(norm_ready, 1)

            turn_affine(hT_hi, hT_lo, KC // UC)
            split_scaling(None)
            latent(0)
            split(KC // UC)
            turn_affine(qlT_hi, qlT_lo, 2)
            latent(1)
            split(1)
            pl.block.n += 1
            for j in range(H * QH // NB):
                split(LORA // P // UC)
                pl.block.n += 1
                if j == 0:
                    turn_affine(kvT_hi, kvT_lo, 2)
            q_blocks = Count()
            q_blocks.n = pl.block.n
            dve.wait_ge(sincos, 1)
            for j in range(2 * D // NB):
                split(LORA // P // UC)
                pl.block.n += 1
                if j == 0:
                    for pair in range(2):
                        dve.wait_ge(pair_read[pair], pair_uses(q_blocks, pair))
                    k2 = kpe[:, :, :].rearrange("p t (f two) -> p t f two", two=2)
                    rope(k2[:, :, :, 0], k2[:, :, :, 1], cos[:, :, :], sin[:, :, :],
                         *(rope_t[:, n, 0:T, :] for n in range(4))).then_inc(q_roped, 1)
                    dve.wait_ge(q_roped, 1)
                if j in (2, 4):
                    t = (j - 2) // 2
                    q2 = mla_q[:, t, :].rearrange("p (h e) -> p h e", e=QH)[:, :, DH:QH]
                    q2 = q2.rearrange("p h (f two) -> p h f two", two=2)
                    cs, sn = (x[:, t, :].unsqueeze(1).to_broadcast([P, H, RH]) for x in (cos, sin))
                    rope(q2[:, :, :, 0], q2[:, :, :, 1], cs, sn,
                         *(rope_t[:, n, :, :] for n in range(4))).then_inc(q_roped, 1)
                    dve.wait_ge(q_roped, 2 + t)
            ada_part(G_A)
            turn_copy(kpT[:, :], lambda b: b[0:ROPE, 0:S])
            turns_written()
            attention(0, MLA_SCALE, mla_mask, True)
            w_o(0)
            layer_norm(0, (0, 0, 0, SH_F, SC_F))
            ffn(0)
            layer_norm(1, (2, 0, 1, SH_A, SC_A))

            turn_affine(hT_hi, hT_lo, KC // UC)
            split_scaling(1)
            split(KC // UC)
            pl.block.n += 2
            ada_part(8)

            def qkv(i):
                split(2 * KC // UC)
                pl.block.n += 2
            loop(dve, 5, pl, qkv, units=2 * KC // UC, blocks=2)
            split(1)
            block_done()
            pair = pl.block.n % 2
            f = [logf[:, n, :, :] for n in range(8)]
            nc.vector.tensor_tensor(f[2], ps[:, 2 * pair:2 * pair + T, 0:H],
                                    bf[:, :].unsqueeze(1).to_broadcast([P, T, H]), ALU.add
                                    ).then_inc(pair_read[pair], 1)
            pl.block.n += 1
            dve.wait_ge(pair_read[pair], pair_uses(pl.block, pair))
            chain(nc.vector.tensor_scalar(f[3], f[2], -1.0, None, ALU.mult))
            nc.vector.tensor_tensor(f[0], f[2], f[3], ALU.max).then_inc(logf_in, 1)
            mark(nc.vector.tensor_scalar(f[7], f[2], 0.0, None, ALU.min))
            dve.wait_ge(expf, 1)
            chain(nc.vector.tensor_scalar(f[3], f[1], 2.0, None, ALU.add))
            chain(nc.vector.reciprocal(f[5], f[3]))
            chain(nc.vector.tensor_tensor(f[4], f[1], f[5], ALU.mult))
            chain(nc.vector.tensor_tensor(f[5], f[4], f[4], ALU.mult))
            chain(nc.vector.tensor_scalar(f[6], f[5], 1.0 / 15, None, ALU.mult))
            for n in (13, 11, 9, 7, 5, 3):
                chain(nc.vector.scalar_tensor_tensor(out=f[6], in0=f[6], scalar=1.0 / n, in1=f[5],
                                                     op0=ALU.add, op1=ALU.mult))
            chain(nc.vector.scalar_tensor_tensor(out=f[6], in0=f[6], scalar=1.0, in1=f[4],
                                                 op0=ALU.add, op1=ALU.mult))
            nc.vector.scalar_tensor_tensor(out=f[7], in0=f[6], scalar=-2.0, in1=f[7],
                                           op0=ALU.mult, op1=ALU.add).then_inc(logf_ready, 1)
            ada_part(9)
            dve.wait_ge(turned, pl.turn.at(1))
            b = ps[0:H, 4 + pl.turn.n % 2, 0:S]
            nc.vector.tensor_scalar(cumT[:, 0, :], b, 1 / FOX_SCALE, None, ALU.mult)
            nc.vector.tensor_scalar(cumT[:, 1, :], b, -1 / FOX_SCALE, None, ALU.mult
                                    ).then_inc(turned_out, 1)
            pl.turn.n += 1
            attention(1, FOX_SCALE, fox_mask, False)
            w_o(1)
            layer_norm(2, (0, 1, 1, SH_F, SC_F))
            ffn(1)
            layer_norm(3)
            for t in range(T):
                scale_xa(t, 3, alpha=1.0)

        @block.tensor
        def _(pe):
            pl = Place()

            def bank_free():
                if pl.turn.i is not None or pl.turn.n >= 2:
                    pe.wait_ge(turned_out, pl.turn.at(-1))

            def turn(tile, c0=0):
                bank_free()
                for c in range(UC):
                    for t in range(T):
                        o = c * S + t * P
                        ins = nc.tensor.transpose(ps[:, 4 + pl.turn.n % 2, o:o + P],
                                                  tile(t, c0 + c), ident[:, :])
                ins.then_inc(turned, 1)
                pl.turn.n += 1

            def reduce_part(acc):
                bank_free()
                for j in range(KC):
                    ins = nc.tensor.matmul(ps[:, 4 + pl.turn.n % 2, j:j + 1],
                                           acc(j * P), ones[:, 0:1],
                                           start=True, stop=True)
                ins.then_inc(turned, 1)
                pl.turn.n += 1

            def reduce_pool(q):
                pe.wait_ge(pool_mac, KC * (POOL_PARTS.index(q) + 1))
                reduce_part(lambda o: ada_acc[:, o:o + P])

            def gate_turns(q):
                pe.wait_ge(turned_out, pl.turn.at())
                for j in range(4):
                    bank_free()
                    for c in range(4):
                        ins = nc.tensor.matmul(ps[:, 4 + pl.turn.n % 2, c * P:(c + 1) * P],
                                               mod[:, q, 4 * j + c:4 * j + c + 1].to_broadcast([P, P]),
                                               ident[:, :], start=True, stop=True)
                    ins.then_inc(turned, 1)
                    pl.turn.n += 1

            def products(chunks, hi, lo, *, per_unit=UC, width=NB, before_unit=None):
                pair = pl.block.n % 2
                if pl.block.n >= 2:
                    pe.wait_ge(pair_read[pair], pair_uses(pl.block, pair))
                for c0 in range(0, chunks, per_unit):
                    if before_unit is not None:
                        before_unit(c0 // per_unit)
                    pe.wait_ge(lo_ready, pl.unit.at(1))
                    s = pl.unit.n % RING
                    for c in range(per_unit):
                        w_hi, w_lo = (x[:, s, c * width:(c + 1) * width] for x in (whi, wlo))
                        for t in range(T):
                            a_hi, a_lo = (x[:, c0 + c, t * P:(t + 1) * P] for x in (hi, lo))
                            o = ps[:, 2 * pair + t, 0:width]
                            first, end = c0 + c == 0, c0 + c == chunks - 1
                            nc.tensor.matmul(o, a_hi, w_hi, start=first, stop=False)
                            nc.tensor.matmul(o, a_hi, w_lo, start=False, stop=False)
                            ins = nc.tensor.matmul(o, a_lo, w_hi, start=False, stop=end)
                    ins.then_inc(units_used, 1)
                    pl.unit.n += 1
                pl.block.n += 1

            def turned_products(tile):
                first = pl.turn.n

                def before(unit):
                    banks = range(0 if unit == 0 else 2 * unit + 1, 2 * unit + 3)
                    for b in banks:
                        if b < KC // UC:
                            turn(tile, UC * b)
                    pe.wait_ge(turned_out, first + unit + 1)
                products(KC, hT_hi, hT_lo, before_unit=before)

            def h_products():
                turned_products(lambda t, c: xa[:, t, c * P:(c + 1) * P])

            def attention(layer, q_tile, qpe_tile, k_tile, v_tile):
                g0 = H * layer
                pe.wait_ge(turned_out, pl.turn.at())
                for pair in range(2):
                    pe.wait_ge(pair_read[pair], pair_uses(pl.block, pair))
                for i in range(H + 3):
                    if i < H:
                        h, g = i, g0 + i
                        if g >= 2:
                            pe.wait_ge(qk_copied, g - 1)
                        for n, tile in enumerate((q_tile, k_tile)):
                            for t in range(T):
                                o = n * S + t * P
                                ins = nc.tensor.transpose(ps[:, g % 2, o:o + P], tile(t, h),
                                                          ident[:, :])
                        ins.then_inc(qk_turned, 1)
                    if 1 <= i <= H:
                        h, g = i - 1, g0 + i - 1
                        pe.wait_ge(qk_copied, g + 1)
                        if qpe_tile is not None:
                            pe.wait_ge(qp_copied, g + 1)
                        if g >= 2:
                            pe.wait_ge(masked, g - 1)
                        for t, a, n in ((0, 0, P), (1, P, S)):
                            o = ps[:, 2 + g % 2, a:a + n]
                            q = slice(t * P, (t + 1) * P)
                            nc.tensor.matmul(o, qkT[:, g % 2, q], qkT[:, g % 2, S:S + n],
                                             start=True, stop=False)
                            if qpe_tile is not None:
                                ins = nc.tensor.matmul(o, qpT[:, g % 2, q], kpT[:, 0:n],
                                                       start=False, stop=True)
                            else:
                                head = ident[0:H, h:h + 1]
                                nc.tensor.matmul(o, head.to_broadcast([H, P]), cumT[:, 1, 0:n],
                                                 start=False, stop=False)
                                ins = nc.tensor.matmul(o, cumT[:, 0, q], head.to_broadcast([H, n]),
                                                       start=False, stop=True)
                        ins.then_inc(scored, 1)
                    if 2 <= i <= H + 1:
                        g = g0 + i - 2
                        pe.wait_ge(exp_done, g + 1)
                        if g >= 2:
                            pe.wait_ge(pT_copied, g - 1)
                        for n in range(3):
                            ins = nc.tensor.transpose(ps[:, 4 + g % 2, n * P:(n + 1) * P],
                                                      p_sb[:, g % 2, n * P:(n + 1) * P], ident[:, :])
                        ins.then_inc(p_turned, 1)
                    if qpe_tile is not None and i < H:
                        if i >= 4:
                            pe.wait_ge(o_scaled, g0 + i - 3)
                        for t in range(T):
                            ins = nc.tensor.transpose(
                                ps[0:ROPE, 6 + (g0 + i) % 2, S + t * P:S + (t + 1) * P],
                                qpe_tile(t, i), ident[:, :])
                        ins.then_inc(qp_turned, 1)
                    if i >= 3:
                        h, g = i - 3, g0 + i - 3
                        pe.wait_ge(pT_copied, g + 1)
                        if g >= 2:
                            pe.wait_ge(o_scaled, g - 1)
                        for q_t, n, k_t in ((0, 0, 0), (1, 1, 0), (1, 2, 1)):
                            ins = nc.tensor.matmul(ps[:, 6 + g % 2, q_t * P:(q_t + 1) * P],
                                                   pT[:, g % 2, n * P:(n + 1) * P], v_tile(k_t, h),
                                                   start=(n < 2), stop=(n != 1))
                        ins.then_inc(pv_done, 1)

            def w_o(layer, o_tile):
                if layer == 0:
                    pe.wait_ge(early_mac, KC)
                    reduce_part(lambda o: gate[:, o:o + P])
                gate_turns(layer * MODS + G_A)
                pe.wait_ge(o_scaled, H * (layer + 1))
                turned_products(o_tile)
                products(KC, hT_hi, hT_lo)
                products(KC, hT_hi, hT_lo)
                products(KC, hT_hi, hT_lo)
                reduce_pool((SH_F, 10)[layer])

            def ffn(l):
                for n, nb in enumerate(FF_PASSES):
                    def turn_u():
                        pair = 1 - pl.block.n % 2
                        pe.wait_ge(pair_read[pair], pair_uses(pl.block, pair))
                        for b in range(2):
                            turn(lambda t, c: u[:, t, c * P:(c + 1) * P], UC * b)

                    def up(i, first=False):
                        if first and n == 0:
                            h_products()
                        else:
                            products(KC, hT_hi, hT_lo)
                        if not first:
                            pair = pl.block.n % 2
                            pe.wait_ge(pair_read[pair], pair_uses(pl.block, pair))
                            for b in range(2):
                                turn(lambda t, c: u[:, t, c * P:(c + 1) * P], UC * b)
                        products(KC, hT_hi, hT_lo)
                    if n == 0:
                        pe.wait_ge(norm_ready, 2 * l + 2)
                    up(0, first=True)
                    loop(pe, nb - 1, pl, up, units=2 * KC // UC, blocks=2, turns=2)

                    def before(unit):
                        if unit == 0 and part_in_down(l, n):
                            reduce_pool(l * MODS + G_F if n == 0 else 7)
                        if unit == 1:
                            turn_u()
                            u_turned.append(pl.turn.n)
                        if unit == 2 and n == 0:
                            gate_turns(l * MODS + G_F)
                        if unit == (4 * nb - 4) // UC:
                            pe.wait_ge(turned_out, u_turned[0])
                    u_turned = []
                    products(4 * nb, uT_hi, uT_lo, before_unit=before)
                    for _ in range(3):
                        products(4 * nb, uT_hi, uT_lo)
                    if l == 0 and n == 0:
                        reduce_pool(6)

            pe.wait_ge(small_in, 16 * n_small)
            pe.wait_ge(consts, n_consts)
            nc.tensor.transpose(ps[:, 4, 0:P], rows[:, 0, :], ident[:, :])
            nc.tensor.transpose(ps[:, 4, P:P + 24], rows[0:24, 1, :], ident[0:24, 0:24])
            n = MODS * KC
            for l in range(LAYERS):
                o = P + 24 + l * n
                ins = nc.tensor.transpose(ps[:, 4, o:o + n], rows[0:n, 2 + l, :], ident[0:n, 0:n])
            ins.then_inc(turned, 1)
            pl.turn.n += 1
            pe.wait_ge(first_mac, 2 * KC)
            for n in range(2):
                reduce_part(lambda o: first_acc[:, n, o:o + P])

            pe.wait_ge(x_in, 16)
            pe.wait_ge(norm_ready, 1)
            h_products()
            products(KC, hT_hi, hT_lo)

            def turn_latent(which):
                pe.wait_ge(pair_read[which], 1)
                for b in range(2):
                    turn(lambda t, c: lat[:, which, t, c * P:(c + 1) * P], UC * b)
            turn_latent(0)
            products(KC, hT_hi, hT_lo, per_unit=KC, width=ROPE)
            for j in range(H * QH // NB):
                if j == 0:
                    pe.wait_ge(turned_out, pl.turn.at())
                products(LORA // P, qlT_hi, qlT_lo)
                if j == 0:
                    turn_latent(1)
            pe.wait_ge(turned_out, pl.turn.at())
            for j in range(2 * D // NB):
                products(LORA // P, kvT_hi, kvT_lo)
            reduce_pool(G_A)
            pe.wait_ge(q_roped, 3)
            bank_free()
            for t in range(T):
                ins = nc.tensor.transpose(ps[0:ROPE, 4 + pl.turn.n % 2, t * P:(t + 1) * P],
                                          kpe[:, t, :], ident[:, :])
            ins.then_inc(turned, 1)
            pl.turn.n += 1
            attention(0, lambda t, h: mla_q[:, t, h * QH:h * QH + DH],
                      lambda t, h: mla_q[:, t, h * QH + DH:(h + 1) * QH],
                      lambda t, h: mla_k[:, t, h * DH:(h + 1) * DH],
                      lambda t, h: mla_v[:, t, h * DH:(h + 1) * DH])
            w_o(0, lambda t, c: mla_v[:, t, c * P:(c + 1) * P])
            ffn(0)

            pe.wait_ge(norm_ready, 3)
            h_products()
            products(KC, hT_hi, hT_lo)
            reduce_pool(8)

            def qkv(i):
                products(KC, hT_hi, hT_lo)
                products(KC, hT_hi, hT_lo)
            loop(pe, 5, pl, qkv, units=2 * KC // UC, blocks=2)
            products(KC, hT_hi, hT_lo, per_unit=KC, width=H)
            reduce_pool(9)
            pe.wait_ge(logf_ready, 1)
            bank_free()
            nc.tensor.matmul(ps[0:H, 4 + pl.turn.n % 2, 0:S], logf[:, 7, 0, :], tri[:, :],
                             start=True, stop=False)
            nc.tensor.matmul(ps[0:H, 4 + pl.turn.n % 2, P:S], logf[:, 7, 1, :], tri[:, 0:P],
                             start=False, stop=True).then_inc(turned, 1)
            pl.turn.n += 1
            attention(1, lambda t, h: fox_qkv[:, t, h * DH:(h + 1) * DH], None,
                      lambda t, h: fox_qkv[:, t, D + h * DH:D + (h + 1) * DH],
                      lambda t, h: fox_qkv[:, t, 2 * D + h * DH:2 * D + (h + 1) * DH])
            w_o(1, lambda t, c: fox_qkv[:, t, 2 * D + c * P:2 * D + (c + 1) * P])
            ffn(1)


_INS = ["x", "c", "positions", "ada_w", "ada_b", "ln1_g", "ln1_b", "ln2_g", "ln2_b",
        "ffn_w1", "ffn_w3", "ffn_w2", "mla_w_down", "mla_q_norm", "mla_w_uq", "mla_kv_norm",
        "mla_w_uk", "mla_w_uv", "mla_w_o", "fox_w_in", "fox_b_f", "fox_w_o"]


def kernel(**inputs):
    from concourse.bacc import Bacc
    from concourse.bass_utils import run_bass_kernel_spmd

    nc = Bacc("TRN2", target_bir_lowering=False, num_devices=1)
    arrays = {name: np.ascontiguousarray(inputs[name]) for name in _INS}
    arrays["inv_freq"] = (np.float32(ROPE_THETA) ** (-np.arange(0, ROPE, 2, dtype=np.float32)
                                                     / np.float32(ROPE))).astype(np.float32)
    A = {name: nc.dram_tensor(f"in_{name}", a.shape, mybir.dt.from_np(a.dtype),
                              kind="ExternalInput").ap() for name, a in arrays.items()}
    out = nc.dram_tensor("out", (1, S, D), F32, kind="ExternalOutput").ap()
    trunk(nc, A, out)
    r = run_bass_kernel_spmd(nc, [{f"in_{n}": a for n, a in arrays.items()}], core_ids=[0])
    return r.results[0]["out"]
```

```python
from contextlib import ExitStack

import numpy as np

import concourse.bass as bass
from concourse import mybir

F32 = mybir.dt.float32
F32R = mybir.dt.float32r
I32 = mybir.dt.int32
ALU = mybir.AluOpType
ACT = mybir.ActivationFunctionType

P = 128
D = 2048
S = 256
T = S // P
KC = D // P
LAYERS = 2
CHUNK = 64
H = 16
DH = 128
LORA = 512
ROPE = 64
RH = ROPE // 2
QH = DH + ROPE
ROPE_THETA = 10000.0
D_FF = -(-8 * D // (3 * 256)) * 256
ALPHA = (2 * LAYERS) ** 0.25
LN_EPS = 1e-5
RMS_EPS = 1e-6
MLA_SCALE = QH ** -0.5
FOX_SCALE = DH ** -0.5
MASKED = -1e30

NB = 512
UC = 2
UNIT = UC * NB
RING = 4
SHIFT = 4
MODS = 6
FF_PASSES = [6, 5]
assert sum(FF_PASSES) * NB == D_FF
U_CHUNKS = max(FF_PASSES) * NB // P
SH_A, SC_A, G_A, SH_F, SC_F, G_F = range(MODS)
assert (SH_A, SC_A) == (0, 1)
QUARTERS = D // NB
QC = KC // QUARTERS
FIRST_SLOTS = 6
EARLY = SC_F
EARLY_UNITS = range(26, 43, 4)
EARLY_LAG = 2
EARLY_REST = 48
POOL_PARTS = [G_A, SH_F, G_F] + [MODS + s for s in range(MODS)]


def early_chunks(unit):
    if unit in EARLY_UNITS:
        return [EARLY_UNITS.index(unit)]
    return range(len(EARLY_UNITS), KC) if unit == EARLY_REST else []


class Count:

    def __init__(self):
        self.n, self.i, self.per, self.start = 0, None, 0, 0

    def at(self, d=0):
        return self.n + d if self.i is None else self.i * self.per + (self.n + d)

    def enter(self, i, per):
        self.i, self.per, self.start = i, per, self.n

    def leave(self, times):
        assert self.n == self.start + self.per, (self.n, self.start, self.per)
        self.n, self.i = self.start + self.per * times, None


class Place:

    def __init__(self):
        self.unit, self.block, self.turn = Count(), Count(), Count()
        self.turn_act, self.step = Count(), Count()

    def all(self):
        return self.unit, self.block, self.turn, self.turn_act, self.step


def loop(eng, times, place, body, *, units=0, blocks=0, turns=0, turns_act=0, steps=0):
    with eng.Fori(0, times) as i:
        for count, per in zip(place.all(), (units, blocks, turns, turns_act, steps)):
            count.enter(i, per)
        body(i)
    for count in place.all():
        count.leave(times)


def two_pi_parts():
    left, parts = 2 * np.pi, []
    for _ in range(4):
        e = int(np.floor(np.log2(left)))
        piece = np.floor(left / 2.0 ** (e - 7)) * 2.0 ** (e - 7)
        parts.append(float(piece))
        left -= piece
    return parts + [float(np.float32(left))]


def trunk(nc, A, out):
    x_d = A["x"][0].rearrange("(t p) d -> p t d", p=P)
    out_d = out[0].rearrange("(t p) d -> p t d", p=P)

    def weight(w):
        return w.rearrange("(c p) n -> p c n", p=P)

    base = -(-nc.sbuf_base // 32) * 32
    at = [base]

    def place_at(name, shape, dt, offset):
        return nc.alloc_sbuf_tensor_at(name, shape, dt, offset=offset)

    def new(name, shape, dt=F32):
        here = at[0]
        at[0] += -(-int(np.prod(shape[1:])) * 4 // 32) * 32
        return place_at(name, shape, dt, here)

    KB = 1024
    a0 = at[0]
    hT_hi = new("hT_hi", [P, KC, S], F32R)
    hT_lo = new("hT_lo", [P, KC, S], F32R)
    mla_k = place_at("mla_k", [P, T, D], F32, a0)
    early_w = place_at("early_w", [P, 2, D], F32, a0 + 16 * KB)
    b0 = at[0]
    at[0] += 48 * KB
    first_w = place_at("first_w", [P, FIRST_SLOTS, D], F32, b0)
    mla_q = place_at("mla_q", [P, T, H * QH], F32, b0)
    mla_v = place_at("mla_v", [P, T, D], F32, b0 + 24 * KB)
    qlT_hi = place_at("qlT_hi", [P, 4, S], F32R, b0 + 24 * KB)
    qlT_lo = place_at("qlT_lo", [P, 4, S], F32R, b0 + 28 * KB)
    lat = place_at("lat", [P, 2, T, LORA], F32, b0 + 32 * KB)
    kvT_hi = place_at("kvT_hi", [P, 4, S], F32R, b0 + 40 * KB)
    kvT_lo = place_at("kvT_lo", [P, 4, S], F32R, b0 + 44 * KB)
    fox_qkv = place_at("fox_qkv", [P, T, 3 * D], F32, b0)
    uT_hi = place_at("uT_hi", [P, U_CHUNKS, S], F32R, b0)
    uT_lo = place_at("uT_lo", [P, U_CHUNKS, S], F32R, b0 + 24 * KB)
    c0 = at[0]
    ln_bc = new("ln_bc", [P, 2, D])
    qkT = place_at("qkT", [P, 2, 2 * S], F32, c0)
    qpT = place_at("qpT", [ROPE, 2, S], F32, c0 + 4 * KB)
    kpT = place_at("kpT", [ROPE, S], F32, c0 + 6 * KB)
    s_sb = place_at("s_sb", [P, 2, 3 * P], F32, c0 + 7 * KB)
    p_sb = place_at("p_sb", [P, 2, 3 * P], F32, c0 + 10 * KB)
    pT = place_at("pT", [P, 2, 3 * P], F32, c0 + 13 * KB)
    rope_t = place_at("rope_t", [P, 4, H, RH], F32, c0 + 8 * KB)
    rows = place_at("rows", [P, 4, P], F32, c0)
    narrow_w = place_at("narrow_w", [P, UNIT], F32, c0 + 4 * KB)
    ang = place_at("ang", [P, 6, T, RH], F32, c0 + 2 * KB)
    silu = place_at("silu", [P, T, NB], F32, c0)
    u = place_at("u", [P, T, NB], F32, c0 + 4 * KB)

    xa = new("xa", [P, T, D])
    gate = new("gate", [P, D])
    ada_acc = new("ada_acc", [P, D])
    ada_w = new("ada_w", [P, 2, D])
    raw = new("raw", [P, RING, UNIT])
    whi = new("whi", [P, RING, UNIT], F32R)
    wlo = new("wlo", [P, RING, UNIT], F32R)
    tmp = new("tmp", [P, 2, NB])
    ident = new("ident", [P, P])
    tri = new("tri", [P, S])
    mla_mask = new("mla_mask", [P, 3 * P])
    fox_mask = new("fox_mask", [P, 3 * P])
    ones = new("ones", [P, 8])
    ln_col = new("ln_col", [P, 4, LAYERS, KC])
    nrm_col = new("nrm_col", [P, 24])
    adab_col = new("adab_col", [P, LAYERS * MODS, KC])
    c_act = new("c_act", [P, KC])
    mod = new("mod", [P, LAYERS * MODS, KC])
    gcol = new("gcol", [P, 2, KC])
    stats = new("stats", [P, T, 4 * 6])
    mv = new("mv", [P, T, 2])
    ssq = new("ssq", [P, 2, T])
    var = new("var", [P, 2])
    root = new("root", [P, 2])
    rstd = new("rstd", [P, 2])
    nt = new("nt", [P, 2])
    nmean = new("nmean", [P, 2])
    cos = new("cos", [P, T, RH])
    sin = new("sin", [P, T, RH])
    inv = new("inv", [P, RH])
    pos_i = new("pos_i", [P, T], I32)
    pos_f = new("pos_f", [P, T])
    kpe = new("kpe", [P, T, ROPE])
    bf = new("bf", [P, H])
    logf = new("logf", [P, 8, T, H])
    cumT = new("cumT", [H, 2, S])
    smax = new("smax", [P, 2, 2])
    nmax = new("nmax", [P, 2, 2])
    psums = new("psums", [P, 2, 2])
    pinv = new("pinv", [P, 2, 2])
    assert at[0] <= nc.sbuf_usable_end, (at[0], nc.sbuf_usable_end)

    with ExitStack() as ctx:
        ps = ctx.enter_context(nc.psum_tensor("ps", [P, 8, NB], F32))

        def sem(name):
            return ctx.enter_context(nc.semaphore(name))

        small_in = sem("small_in")
        x_in = sem("x_in")
        first_in = [sem(f"first_in{i}") for i in range(FIRST_SLOTS)]
        early_in = [sem(f"early_in{i}") for i in range(2)]
        raw_in = [sem(f"raw_in{i}") for i in range(RING)]
        narrow_in = sem("narrow_in")
        ada_in = [sem(f"ada_in{i}") for i in range(2)]
        ln_in = sem("ln_in")
        out_done = sem("out_done")
        consts = sem("consts")
        hi_ready = sem("hi_ready")
        lo_ready = sem("lo_ready")
        units_used = sem("units_used")
        pair_read = [sem(f"pair_read{i}") for i in range(2)]
        turned = sem("turned")
        turned_act = sem("turned_act")
        turned_out = sem("turned_out")
        dve_step = sem("dve_step")
        act_step = sem("act_step")
        pool_mac = sem("pool_mac")
        pool_prod = sem("pool_prod")
        chunk_seen = sem("chunk_seen")
        first_mac = sem("first_mac")
        early_mac = sem("early_mac")
        acc_reduced = sem("acc_reduced")
        c_ready = sem("c_ready")
        angles = sem("angles")
        sincos = sem("sincos")
        ssq_ready = sem("ssq_ready")
        root_ready = sem("root_ready")
        rstd_ready = sem("rstd_ready")
        lat_ready = sem("lat_ready")
        var_ready = sem("var_ready")
        gcol_ready = sem("gcol_ready")
        nmean_ready = sem("nmean_ready")
        norm_ready = sem("norm_ready")
        norm_act = sem("norm_act")
        xa_updated = sem("xa_updated")
        q_roped = sem("q_roped")
        logf_ready = sem("logf_ready")
        logf_in = sem("logf_in")
        expf = sem("expf")
        qk_turned = sem("qk_turned")
        qk_copied = sem("qk_copied")
        qp_turned = sem("qp_turned")
        qp_copied = sem("qp_copied")
        scored = sem("scored")
        masked = sem("masked")
        max_ready = sem("max_ready")
        exp_done = sem("exp_done")
        p_turned = sem("p_turned")
        pT_copied = sem("pT_copied")
        pv_done = sem("pv_done")
        o_scaled = sem("o_scaled")
        out_ready = sem("out_ready")

        block = ctx.enter_context(nc.Block())

        n_small = 13
        n_consts = 5 + 2 + 4

        def flat(tile):
            return tile[:, :, :].rearrange("p c s -> p (c s)")

        def part_in_down(l, n):
            return l == 0 or n == 0

        def pair_uses(b, p):
            n = (b.n + 1 - p) // 2
            return n if b.i is None else b.i * (b.per // 2) + n

        narrow_units = {}

        def unit_loads(unit):
            narrow = sum(m < unit.n and m % RING == unit.n % RING for m in narrow_units)
            n = 16 * (unit.n // RING + 1 - narrow)
            return n if unit.i is None else unit.i * (16 * unit.per // RING) + n

        def source(unit):
            if unit.i is None and unit.n in narrow_units:
                return narrow_w, narrow_units[unit.n]
            return raw, UNIT

        def narrow_load(unit):
            return 16 * (1 + sum(m < unit.n for m in narrow_units))

        @block.sync
        def _(sp):
            pl = Place()

            def small(dst, src):
                sp.dma_start(dst, src).then_inc(small_in, 16)

            for r, name in enumerate(("ln1_g", "ln1_b", "ln2_g", "ln2_b")):
                small(rows[r * 32:(r + 1) * 32, 0, :], A[name].rearrange("l (c p) -> (l c) p", p=P))
            small(rows[0:KC, 1, :], A["c"].rearrange("b (c p) -> (b c) p", p=P))
            small(rows[KC:KC + 4, 1, :], A["mla_q_norm"].rearrange("b (c p) -> (b c) p", p=P))
            small(rows[KC + 4:KC + 8, 1, :], A["mla_kv_norm"].rearrange("b (c p) -> (b c) p", p=P))
            for l in range(LAYERS):
                small(rows[0:MODS * KC, 2 + l, :], A["ada_b"][l].rearrange("(c p) -> c p", p=P))
            for t in range(T):
                small(pos_i[:, t:t + 1],
                      A["positions"][0, t * P:(t + 1) * P].rearrange("(p a) -> p a", a=1))
            small(inv[:, :], A["inv_freq"].partition_broadcast(P))
            small(bf[:, :], A["fox_b_f"][0].partition_broadcast(P))

            def load_narrow(w, col, width):
                dst = narrow_w[:, 0:KC * width].rearrange("p (c n) -> p c n", c=KC)
                sp.dma_start(dst, w[:, :, col:col + width]).then_inc(narrow_in, 16)

            down = weight(A["mla_w_down"][0])
            def load_early(m):
                if m < 2:
                    sp.wait_ge(units_used, 2 * KC // UC + 1)
                else:
                    sp.wait_ge(early_mac, m - 1)
                sp.dma_start(early_w[:, m % 2, :],
                             A["ada_w"][0, m * P:(m + 1) * P, EARLY * D:(EARLY + 1) * D]
                             ).then_inc(early_in[m % 2], 16)

            def load(w, chunk, col):
                s = pl.unit.n % RING
                if pl.unit.i is not None or pl.unit.n >= RING:
                    sp.wait_ge(lo_ready, pl.unit.at(1 - RING))
                dst = raw[:, s, :].rearrange("p (c n) -> p c n", c=UC)
                sp.dma_start(dst, w[:, chunk:chunk + UC, bass.ds(col, NB)]
                             ).then_inc(raw_in[s], 16)
                if pl.unit.i is None:
                    for m in early_chunks(pl.unit.n):
                        load_early(m)
                pl.unit.n += 1

            ada_first = weight(A["ada_w"][0])[:, :, 0:2 * D].rearrange("p k (a d) -> p k a d", a=2)
            pairs = KC // 2
            for n in range(QUARTERS * pairs):
                j, m, slot = n // pairs, n % pairs, n % FIRST_SLOTS
                if n >= FIRST_SLOTS:
                    sp.wait_ge(first_mac, 2 * (n - FIRST_SLOTS + 1))
                for k in range(2):
                    dst = first_w[:, slot, k * 2 * NB:(k + 1) * 2 * NB]
                    sp.dma_start(dst.rearrange("p (a n) -> p a n", a=2),
                                 ada_first[:, 2 * m + k, :, j * NB:(j + 1) * NB]
                                 ).then_inc(first_in[slot], 16)
                if n == FIRST_SLOTS - 1:
                    sp.dma_start(xa[:, :, :], x_d).then_inc(x_in, 16)
                if m == pairs - 1:
                    for col in (0, LORA):
                        for c in range(0, QC, UC):
                            load(down, j * QC + c, col)

            def narrow(width):
                narrow_units[pl.unit.n] = KC * width
                pl.unit.n += 1

            def load_block(w, col, chunk0, chunks):
                for c in range(0, chunks, UC):
                    load(w, chunk0 + c, col)

            def load_ln(k, names, layer):
                if k % 2 == 0:
                    sp.wait_ge(o_scaled, H * (layer + 1))
                else:
                    sp.wait_ge(units_used, pl.unit.at(SHIFT - 4 * (FF_PASSES[-1] * NB // P) // UC))
                for j, name in enumerate(names):
                    sp.dma_start(ln_bc[:, j, :], A[name][layer].partition_broadcast(P)
                                 ).then_inc(ln_in, 16)

            def load_wo(w):
                loop(sp, 2, pl, lambda i: [load_block(w, i * (2 * NB) + j * NB, 0, KC)
                                           for j in range(2)], units=2 * KC // UC)

            def load_ffn(l):
                w1, w3, w2 = (weight(A[n][l]) for n in ("ffn_w1", "ffn_w3", "ffn_w2"))
                first = 0
                for nb in FF_PASSES:
                    def up(i):
                        load_block(w1, i * NB + first * NB, 0, KC)
                        load_block(w3, i * NB + first * NB, 0, KC)
                    loop(sp, nb, pl, up, units=2 * KC // UC)
                    loop(sp, 2, pl, lambda i: [load_block(w2, i * (2 * NB) + j * NB, 4 * first, 4 * nb)
                                               for j in range(2)], units=2 * 4 * nb // UC)
                    first += nb

            load_narrow(down, 2 * LORA, ROPE)
            narrow(ROPE)
            for name, cols in (("mla_w_uq", H * QH), ("mla_w_uk", D), ("mla_w_uv", D)):
                for col in range(0, cols, NB):
                    load_block(weight(A[name][0]), col, 0, LORA // P)
            for col in range(0, D, NB):
                load_block(weight(A["mla_w_o"][0]), col, 0, KC)
            load_ln(0, ("ln1_g", "ln1_b"), 0)
            load_ffn(0)
            load_ln(1, ("ln2_g", "ln2_b"), 0)
            w_in = weight(A["fox_w_in"][0])
            load_block(w_in, 0, 0, KC)
            load_block(w_in, NB, 0, KC // 2)
            sp.wait_ge(xa_updated, 2)
            load_narrow(w_in, 3 * D, H)
            load_block(w_in, NB, KC // 2, KC // 2)
            narrow(H)
            loop(sp, 5, pl, lambda i: [load_block(w_in, i * (2 * NB) + (2 + j) * NB, 0, KC)
                                       for j in range(2)], units=2 * KC // UC)
            load_wo(weight(A["fox_w_o"][0]))
            load_ln(2, ("ln1_g", "ln1_b"), 1)
            load_ffn(1)
            load_ln(3, ("ln2_g", "ln2_b"), 1)
            for t in range(T):
                sp.wait_ge(out_ready, t + 1)
                sp.dma_start(out_d[:, t, :], xa[:, t, :]).then_inc(out_done, 16)
            sp.wait_ge(out_done, 16 * T)

        @block.gpsimd
        def _(pool):
            nc.gpsimd.memset(ones[:, :], 1.0).then_inc(consts, 1)
            nc.gpsimd.memset(ident[:, :], 0.0).then_inc(consts, 1)
            nc.gpsimd.memset(tri[:, :], 1.0).then_inc(consts, 1)
            nc.gpsimd.memset(mla_mask[:, :], 0.0).then_inc(consts, 1)
            nc.gpsimd.memset(fox_mask[:, :], 0.0).then_inc(consts, 1)
            pool.wait_ge(consts, 5)
            nc.gpsimd.affine_select(out=ident[:, :], in_=ident[:, :], compare_op=ALU.not_equal,
                                    fill=1.0, base=0, pattern=[[-1, P]],
                                    channel_multiplier=1).then_inc(consts, 1)
            nc.gpsimd.affine_select(out=tri[:, 0:P], in_=tri[:, 0:P], compare_op=ALU.is_ge,
                                    fill=0.0, base=0, pattern=[[1, P]],
                                    channel_multiplier=-1).then_inc(consts, 1)
            for o in (0, 2 * P):
                nc.gpsimd.memset(mla_mask[0:CHUNK, o + CHUNK:o + P], MASKED).then_inc(consts, 1)
                nc.gpsimd.affine_select(out=fox_mask[:, o:o + P], in_=fox_mask[:, o:o + P],
                                        compare_op=ALU.is_ge, fill=MASKED, base=0,
                                        pattern=[[-1, P]], channel_multiplier=1).then_inc(consts, 1)

            def part(layer, s, r):
                for k in range(KC + 1):
                    if k < KC:
                        if k >= 2 or not isinstance(r, int) or r > 0:
                            pool.wait_ge(pool_mac, r * KC + (k - 1))
                        pool.dma_start(ada_w[:, k % 2, :],
                                       A["ada_w"][layer, k * P:(k + 1) * P, bass.ds(s * D, D)]
                                       ).then_inc(ada_in[k % 2], 16)
                    if k == 0:
                        continue
                    j = k - 1
                    w = ada_w[:, j % 2, :]
                    pool.wait_ge(ada_in[j % 2], r * (8 * KC) + 16 * (j // 2 + 1))
                    pool.sem_inc(chunk_seen, 1)
                    if j == 0:
                        nc.gpsimd.tensor_scalar(ada_acc[:, :], w, c_act[:, 0:1], 0.0,
                                                ALU.mult, ALU.add).then_inc(pool_mac, 1)
                        continue
                    nc.gpsimd.tensor_scalar(w, w, c_act[:, j:j + 1], 0.0,
                                            ALU.mult, ALU.add).then_inc(pool_prod, 1)
                    pool.wait_ge(pool_prod, r * (KC - 1) + j)
                    pool.wait_ge(pool_mac, r * KC + j)
                    nc.gpsimd.tensor_tensor(ada_acc[:, :], ada_acc[:, :], w, ALU.add
                                            ).then_inc(pool_mac, 1)

            pool.wait_ge(first_mac, QUARTERS * KC - 28)
            part(0, G_A, 0)
            pool.wait_ge(acc_reduced, 1)
            part(0, SH_F, 1)
            pool.wait_ge(acc_reduced, 3)
            part(0, G_F, 2)
            with pool.Fori(0, MODS) as s:
                pool.wait_ge(acc_reduced, s + 4)
                part(1, s, s + 3)

        @block.scalar
        def _(act):
            pl = Place()

            def split(n):
                for _ in range(n):
                    s = pl.unit.n % RING
                    src, n = source(pl.unit)
                    if src is narrow_w:
                        act.wait_ge(narrow_in, narrow_load(pl.unit))
                    else:
                        act.wait_ge(raw_in[s], unit_loads(pl.unit))
                    if pl.unit.i is not None or pl.unit.n >= RING:
                        act.wait_ge(units_used, pl.unit.at(1 - RING))
                    src = src[:, 0:n] if src is narrow_w else src[:, s, :]
                    nc.scalar.activation(whi[:, s, 0:n], src, ACT.Copy).then_inc(hi_ready, 1)
                    pl.unit.n += 1

            def block_done():
                act.wait_ge(units_used, pl.unit.at(-SHIFT))

            def free_pair(ins):
                ins.then_inc(pair_read[pl.block.n % 2], 1)
                pl.block.n += 1

            def copy_block(dst):
                block_done()
                p = 2 * (pl.block.n % 2)
                for t in range(T):
                    ins = nc.scalar.activation(dst(t), ps[:, p + t, :], ACT.Copy)
                free_pair(ins)

            def turn_affine(banks, gain, offset=None, first=0):
                for b in range(first, first + banks):
                    act.wait_ge(turned, pl.turn.at(1))
                    act.wait_ge(turned_out, pl.turn.at(-1))
                    for c in range(UC):
                        i, o = (x[:, c * S:(c + 1) * S] for x in (ps[:, 4 + pl.turn.n % 2, :],
                                                                  tmp[:, pl.turn.n % 2, :]))
                        if offset is None:
                            ins = nc.scalar.activation(o, i, ACT.Copy, scale=gain(UC * b + c))
                        else:
                            ins = nc.scalar.activation(o, i, ACT.Identity, scale=gain(UC * b + c),
                                                       bias=offset(UC * b + c))
                    ins.then_inc(turned_act, 1)
                    pl.turn.n += 1
                    pl.turn_act.n += 1

            def turn_plain(dst, chunk, banks):
                for b in range(banks):
                    act.wait_ge(turned, pl.turn.at(1))
                    nc.scalar.activation(flat(dst)[:, bass.ds(chunk * S + UC * b * S, UC * S)],
                                         ps[:, 4 + pl.turn.n % 2, :], ACT.Copy
                                         ).then_inc(turned_act, 1)
                    pl.turn.n += 1
                    pl.turn_act.n += 1

            def h_turns(banks=KC // UC, first=0):
                turn_affine(banks, lambda c: gcol[:, 0, c:c + 1], lambda c: gcol[:, 1, c:c + 1],
                            first)

            def take_root(norm):
                act.wait_ge(var_ready, norm + 1)
                nc.scalar.activation(root[:, :], var[:, :], ACT.Sqrt).then_inc(root_ready, 1)

            def layer_norm(k):
                take_root(2 + k)
                act.wait_ge(nmean_ready, k + 1)
                nc.scalar.activation(xa[:, 1, :], xa[:, 1, :], ACT.Identity, scale=rstd[:, 1:2],
                                     bias=nmean[:, 1:2]).then_inc(norm_act, 1)

            def latent(which):
                block_done()
                act.wait_ge(turned_out, pl.turn.at())
                p = 2 * (pl.block.n % 2)
                for t in range(T):
                    ins = nc.scalar.activation(tmp[:, t, :], ps[:, p + t, :], ACT.Square,
                                               accum_out=ssq[:, which, t:t + 1])
                ins.then_inc(ssq_ready, 1)
                take_root(which)
                act.wait_ge(rstd_ready, which + 1)
                for t in range(T):
                    ins = nc.scalar.activation(lat[:, which, t, :], ps[:, p + t, :], ACT.Copy,
                                               scale=rstd[:, t:t + 1])
                free_pair(ins)

            def attention(layer, scale, out_tile):
                g0 = H * layer
                for i in range(H + 3):
                    if i < H:
                        g = g0 + i
                        act.wait_ge(qk_turned, g + 1)
                        if g >= 2:
                            act.wait_ge(scored, g - 1)
                        nc.scalar.activation(qkT[:, g % 2, :], ps[:, g % 2, :], ACT.Copy
                                             ).then_inc(qk_copied, 1)
                    if 1 <= i <= H:
                        g = g0 + i - 1
                        act.wait_ge(max_ready, g + 1)
                        if g >= 2:
                            act.wait_ge(pT_copied, g - 1)
                        for t, a, b in ((0, 0, P), (1, P, 3 * P)):
                            ins = nc.scalar.activation(p_sb[:, g % 2, a:b], s_sb[:, g % 2, a:b],
                                                       ACT.Exp, bias=nmax[:, g % 2, t:t + 1],
                                                       scale=scale,
                                                       accum_out=psums[:, g % 2, t:t + 1])
                        ins.then_inc(exp_done, 1)
                    if i >= 3:
                        g = g0 + i - 3
                        act.wait_ge(pv_done, g + 1)
                        for t in range(T):
                            ins = nc.scalar.activation(out_tile(t, i - 3),
                                                       ps[:, 6 + g % 2, t * P:(t + 1) * P],
                                                       ACT.Copy, scale=pinv[:, g % 2, t:t + 1])
                        ins.then_inc(o_scaled, 1)

            def w_o(layer):
                pl.turn.n += (1 - layer) + 4
                turn_plain(hT_hi, 0, KC // UC)

                def body(i):
                    split(2 * KC // UC)
                    pl.block.n += 2
                loop(act, 2, pl, body, units=2 * KC // UC, blocks=2)
                pl.turn.n += 1

            def ffn(l):
                for n, nb in enumerate(FF_PASSES):
                    def up(i, first=False):
                        split(KC // UC)
                        block_done()
                        pair = pl.block.n % 2
                        if first and n == 0:
                            act.wait_ge(xa_updated, 2 * l + 1)
                        act.wait_ge(pair_read[1 - pair], pair_uses(pl.block, 1 - pair))
                        for t in range(T):
                            ins = nc.scalar.activation(silu[:, t, :], ps[:, 2 * pair + t, :],
                                                       ACT.Silu)
                        free_pair(ins)
                        if not first:
                            turn_plain(uT_hi, i * 4, 2)
                        split(KC // UC)
                        pl.block.n += 1
                    if n == 0:
                        h_turns()
                    up(0, first=True)
                    loop(act, nb - 1, pl, up, units=2 * KC // UC, blocks=2, turns=2, turns_act=2)
                    with_part, with_gate = part_in_down(l, n), n == 0
                    pl.turn.n += with_part
                    turn_plain(uT_hi, 4 * (nb - 1), 2)
                    pl.turn.n += 4 * with_gate
                    end = l == LAYERS - 1 and n == len(FF_PASSES) - 1
                    split(4 * 4 * nb // UC - SHIFT * end)
                    pl.block.n += 4
                    if l == 0 and n == 0:
                        pl.turn.n += 1

            act.wait_ge(turned_out, 1)
            nc.scalar.activation(c_act[:, :], nrm_col[:, 0:KC], ACT.Silu).then_inc(c_ready, 1)
            act.wait_ge(angles, 1)
            nc.scalar.activation(sin[:, :, :], ang[:, 4, :, :], ACT.Sin)
            nc.scalar.activation(cos[:, :, :], ang[:, 5, :, :], ACT.Sin).then_inc(sincos, 1)
            pl.turn.n += 1

            for j in range(QUARTERS):
                split(2 * QC // UC)
                pl.turn.n += 1
                h_turns(QC // UC, j * QC // UC)
            split(SHIFT - QC // UC)
            latent(0)
            split(QC // UC)
            turn_affine(2, lambda c: nrm_col[:, KC + c:KC + c + 1])
            latent(1)
            split(1)
            block_done()
            free_pair(nc.scalar.activation(kpT[:, :], ps[0:ROPE, 2 * (pl.block.n % 2), 0:S],
                                           ACT.Copy))
            for j in range(H * QH // NB):
                split(LORA // P // UC)
                copy_block(lambda t: mla_q[:, t, j * NB:(j + 1) * NB])
                if j == 0:
                    turn_affine(2, lambda c: nrm_col[:, KC + 4 + c:KC + 5 + c])
                    pl.turn.n += 1
            for dst in (mla_k, mla_v):
                for j in range(D // NB):
                    split(LORA // P // UC)
                    copy_block(lambda t: dst[:, t, j * NB:(j + 1) * NB])
            pl.turn.n += 2
            attention(0, MLA_SCALE, lambda t, h: mla_v[:, t, h * DH:(h + 1) * DH])
            w_o(0)
            layer_norm(0)
            ffn(0)
            layer_norm(1)

            h_turns()

            def qkv(i, lead=0):
                for j in range(2):
                    split(KC // UC)
                    copy_block(lambda t: fox_qkv[:, t, bass.ds(i * (2 * NB) + (lead + j) * NB, NB)])
            qkv(0)
            pl.turn.n += 1
            split(1)
            pl.block.n += 1
            pl.turn.n += 1
            act.wait_ge(logf_in, 1)
            nc.scalar.activation(logf[:, 1, :, :], logf[:, 0, :, :], ACT.Exp, scale=-1.0
                                 ).then_inc(expf, 1)
            loop(act, 5, pl, lambda i: qkv(i, 2), units=2 * KC // UC, blocks=2)
            pl.turn.n += 2
            attention(1, FOX_SCALE, lambda t, h: fox_qkv[:, t, 2 * D + h * DH:2 * D + (h + 1) * DH])
            w_o(1)
            layer_norm(2)
            ffn(1)
            layer_norm(3)

        @block.vector
        def _(dve):
            pl = Place()

            def mark(ins):
                ins.then_inc(dve_step, 1)
                pl.step.n += 1

            def own():
                dve.wait_ge(dve_step, pl.step.at())

            def chain(ins):
                mark(ins)
                own()

            def split(n):
                for _ in range(n):
                    s = pl.unit.n % RING
                    dve.wait_ge(hi_ready, pl.unit.at(1))
                    src, n = source(pl.unit)
                    src = src[:, 0:n] if src is narrow_w else src[:, s, :]
                    nc.vector.tensor_tensor(wlo[:, s, 0:n], src, whi[:, s, 0:n].bitcast(F32),
                                            ALU.subtract).then_inc(lo_ready, 1)
                    if pl.unit.i is None:
                        for m in early_chunks(pl.unit.n - EARLY_LAG):
                            early_part(m)
                    pl.unit.n += 1

            def early_part(m):
                dve.wait_ge(early_in[m % 2], 16 * (m // 2 + 1))
                if m == 0:
                    ins = nc.vector.tensor_scalar(gate[:, :], early_w[:, 0, :], c_act[:, 0:1],
                                                  None, ALU.mult)
                else:
                    dve.wait_ge(early_mac, m)
                    ins = nc.vector.scalar_tensor_tensor(out=gate[:, :], in0=early_w[:, m % 2, :],
                                                         scalar=c_act[:, m:m + 1], in1=gate[:, :],
                                                         op0=ALU.mult, op1=ALU.add)
                ins.then_inc(early_mac, 1)

            def block_done():
                dve.wait_ge(units_used, pl.unit.at(-SHIFT))

            def turn_affine(hi, lo, banks, first=0):
                for b in range(first, first + banks):
                    dve.wait_ge(turned_act, pl.turn_act.at(1))
                    o = slice(b * UC * S, (b + 1) * UC * S)
                    src = tmp[:, pl.turn.n % 2, :]
                    chain(nc.vector.tensor_copy(flat(hi)[:, o], src))
                    nc.vector.tensor_tensor(flat(lo)[:, o], src, flat(hi)[:, o].bitcast(F32),
                                            ALU.subtract).then_inc(turned_out, 1)
                    pl.turn.n += 1
                    pl.turn_act.n += 1

            def turn_plain(hi, lo, chunk, banks):
                for b in range(banks):
                    dve.wait_ge(turned_act, pl.turn_act.at(1))
                    o = bass.ds(chunk * S + UC * b * S, UC * S)
                    nc.vector.tensor_tensor(flat(lo)[:, o], ps[:, 4 + pl.turn.n % 2, :],
                                            flat(hi)[:, o].bitcast(F32), ALU.subtract
                                            ).then_inc(turned_out, 1)
                    pl.turn.n += 1
                    pl.turn_act.n += 1

            def turn_copy(dst, src):
                dve.wait_ge(turned, pl.turn.at(1))
                nc.vector.tensor_copy(dst, src(ps[:, 4 + pl.turn.n % 2, :])).then_inc(turned_out, 1)
                pl.turn.n += 1

            def turns_written():
                dve.wait_ge(turned_out, pl.turn.at())

            def ada_part(q):
                dve.wait_ge(turned, pl.turn.at(1))
                plus = 1.0 if q % MODS in (SC_A, G_A, SC_F, G_F) else 0.0
                for half, done in ((slice(0, KC // 2), acc_reduced), (slice(KC // 2, KC), turned_out)):
                    nc.vector.scalar_tensor_tensor(out=mod[:, q, half],
                                                   in0=ps[:, 4 + pl.turn.n % 2, half], scalar=plus,
                                                   in1=adab_col[:, q, half], op0=ALU.add,
                                                   op1=ALU.add).then_inc(done, 1)
                pl.turn.n += 1
                turns_written()

            def gate_in():
                for j in range(4):
                    turn_copy(gate[:, j * NB:(j + 1) * NB], lambda b: b)
                turns_written()

            def newton(norm):
                dve.wait_ge(root_ready, norm + 1)
                chain(nc.vector.reciprocal(rstd[:, :], root[:, :]))
                chain(nc.vector.tensor_tensor(nt[:, :], rstd[:, :], rstd[:, :], ALU.mult))
                chain(nc.vector.tensor_tensor(nt[:, :], nt[:, :], var[:, :], ALU.mult))
                chain(nc.vector.tensor_scalar(nt[:, :], nt[:, :], -0.5, 1.5, ALU.mult, ALU.add))
                return nc.vector.tensor_tensor(rstd[:, :], rstd[:, :], nt[:, :], ALU.mult)

            def latent(which):
                dve.wait_ge(ssq_ready, which + 1)
                nc.vector.tensor_scalar(var[:, :], ssq[:, which, :], 1.0 / LORA, RMS_EPS,
                                        ALU.mult, ALU.add).then_inc(var_ready, 1)
                newton(which).then_inc(rstd_ready, 1)
                pl.block.n += 1

            def residual(col, stat_col, last):
                block_done()
                pair = pl.block.n % 2
                own()
                for t in range(T):
                    ins = nc.vector.tensor_tensor(tmp[:, t, :], ps[:, 2 * pair + t, :],
                                                  gate[:, bass.ds(col, NB)], ALU.mult)
                ins.then_inc(pair_read[pair], 1)
                pl.block.n += 1
                dve.wait_ge(pair_read[pair], pair_uses(pl.block, pair))
                for t in range(T):
                    mark(nc.vector.tensor_tensor(xa[:, t, bass.ds(col, NB)],
                                                 xa[:, t, bass.ds(col, NB)], tmp[:, t, :],
                                                 ALU.add))
                if last:
                    own()
                    for t in range(T):
                        mark(nc.vector.bn_stats(stats[:, t, bass.ds(stat_col, 6)],
                                                xa[:, t, bass.ds(col, NB)]))

            def affine_cols(cols, layer, to_layer, sh, sc):
                q = to_layer * MODS
                chain(nc.vector.tensor_tensor(gcol[:, 0, :], ln_col[:, cols, layer, :],
                                              mod[:, q + sc, :], ALU.mult))
                chain(nc.vector.tensor_tensor(gcol[:, 1, :], ln_col[:, cols + 1, layer, :],
                                              mod[:, q + sc, :], ALU.mult))
                chain(nc.vector.tensor_tensor(gcol[:, 1, :], gcol[:, 1, :], mod[:, q + sh, :],
                                              ALU.add))

            def layer_norm(k, cols=None):
                own()
                for t in range(T):
                    mark(nc.vector.bn_aggr(mv[:, t, :], stats[:, t, :]))
                own()
                nc.vector.tensor_scalar(var[:, :], mv[:, :, 1], LN_EPS, None, ALU.add
                                        ).then_inc(var_ready, 1)
                if cols is not None:
                    affine_cols(*cols)
                chain(newton(2 + k))
                nc.vector.scalar_tensor_tensor(out=nmean[:, :], in0=mv[:, :, 0], scalar=-1.0,
                                               in1=rstd[:, :], op0=ALU.mult, op1=ALU.mult
                                               ).then_inc(nmean_ready, 1)
                dve.wait_ge(nmean_ready, k + 1)
                nc.vector.tensor_scalar(xa[:, 0, :], xa[:, 0, :], rstd[:, 0:1],
                                        nmean[:, 0:1], ALU.mult, ALU.add).then_inc(norm_ready, 1)
                dve.wait_ge(norm_ready, k + 1)
                dve.wait_ge(norm_act, k + 1)

            def scale_xa(t, k, alpha=ALPHA):
                if k is None:
                    mark(nc.vector.tensor_scalar(xa[:, t, :], xa[:, t, :], alpha, None, ALU.mult))
                    return
                dve.wait_ge(ln_in, 32 * (k + 1))
                chain(nc.vector.scalar_tensor_tensor(out=xa[:, t, :], in0=xa[:, t, :], scalar=alpha,
                                                     in1=ln_bc[:, 0, :], op0=ALU.mult,
                                                     op1=ALU.mult))
                ins = nc.vector.scalar_tensor_tensor(out=xa[:, t, :], in0=ln_bc[:, 1, :],
                                                     scalar=alpha, in1=xa[:, t, :], op0=ALU.mult,
                                                     op1=ALU.add)
                if alpha == 1.0:
                    ins.then_inc(out_ready, 1)
                    return
                if t == T - 1:
                    ins.then_inc(xa_updated, 1)
                    dve.wait_ge(xa_updated, k + 1)
                else:
                    mark(ins)

            def split_scaling(k):
                for t in range(T):
                    split(KC // UC // T)
                    scale_xa(t, k)

            def rope(x0, x1, cs, sn, t0, t1, t2, t3):
                mark(nc.vector.tensor_tensor(t0, x0, cs, ALU.mult))
                mark(nc.vector.tensor_tensor(t1, x1, sn, ALU.mult))
                mark(nc.vector.tensor_tensor(t2, x0, sn, ALU.mult))
                mark(nc.vector.tensor_tensor(t3, x1, cs, ALU.mult))
                own()
                mark(nc.vector.tensor_tensor(x0, t0, t1, ALU.subtract))
                return nc.vector.tensor_tensor(x1, t2, t3, ALU.add)

            def attention(layer, scale, mask, rotary):
                g0 = H * layer
                for i in range(H + 2):
                    if 1 <= i <= H:
                        g = g0 + i - 1
                        dve.wait_ge(scored, g + 1)
                        if g >= 2:
                            dve.wait_ge(exp_done, g - 1)
                        for t, a, b in ((0, 0, P), (1, P, 3 * P)):
                            ins = nc.vector.tensor_tensor_reduce(
                                s_sb[:, g % 2, a:b], ps[:, 2 + g % 2, a:b], mask[:, a:b], 1.0,
                                -3.0e38, ALU.add, ALU.max, smax[:, g % 2, t:t + 1])
                        ins.then_inc(masked, 1)
                        dve.wait_ge(masked, g + 1)
                        nc.vector.tensor_scalar(nmax[:, g % 2, :], smax[:, g % 2, :], -scale, None,
                                                ALU.mult).then_inc(max_ready, 1)
                    if rotary and i < H:
                        g = g0 + i
                        dve.wait_ge(qp_turned, g + 1)
                        if g >= 2:
                            dve.wait_ge(scored, g - 1)
                        nc.vector.tensor_copy(qpT[:, g % 2, :], ps[0:ROPE, 6 + g % 2, S:2 * S]
                                              ).then_inc(qp_copied, 1)
                    if i >= 2:
                        g = g0 + i - 2
                        dve.wait_ge(p_turned, g + 1)
                        if g >= 2:
                            dve.wait_ge(o_scaled, g - 1)
                        nc.vector.reciprocal(pinv[:, g % 2, :], psums[:, g % 2, :])
                        nc.vector.tensor_copy(pT[:, g % 2, :], ps[:, 4 + g % 2, 0:3 * P]
                                              ).then_inc(pT_copied, 1)
                    if layer == 0 and i >= 1 and len(EARLY_UNITS) + i - 1 < KC:
                        early_part(len(EARLY_UNITS) + i - 1)

            def w_o(layer):
                if layer == 0:
                    ada_part(EARLY)
                gate_in()
                turn_plain(hT_hi, hT_lo, 0, KC // UC)

                def body(i):
                    for j in range(2):
                        split(KC // UC)
                        residual(i * (2 * NB) + j * NB, i * 12 + j * 6, True)
                loop(dve, 2, pl, body, units=2 * KC // UC, blocks=2, steps=8)
                ada_part((SH_F, 10)[layer])

            def ffn(l):
                for n, nb in enumerate(FF_PASSES):
                    last = n == len(FF_PASSES) - 1

                    def up(i, first=False):
                        if first and n == 0:
                            split_scaling(2 * l)
                        else:
                            split(KC // UC)
                        if not first:
                            turn_plain(uT_hi, uT_lo, i * 4, 2)
                        split(KC // UC)
                        pl.block.n += 1
                        block_done()
                        pair = pl.block.n % 2
                        dve.wait_ge(pair_read[1 - pair], pair_uses(pl.block, 1 - pair))
                        for t in range(T):
                            ins = nc.vector.tensor_tensor(u[:, t, :], silu[:, t, :],
                                                          ps[:, 2 * pair + t, :], ALU.mult)
                        ins.then_inc(pair_read[pair], 1)
                        pl.block.n += 1
                    if n == 0:
                        turn_affine(hT_hi, hT_lo, KC // UC)
                    up(0, first=True)
                    loop(dve, nb - 1, pl, up, units=2 * KC // UC, blocks=2, turns=2, turns_act=2)
                    if part_in_down(l, n):
                        ada_part(l * MODS + G_F if n == 0 else 7)
                    turn_plain(uT_hi, uT_lo, 4 * (nb - 1), 2)
                    if n == 0:
                        gate_in()
                    nu = 4 * nb // UC
                    for j in range(4):
                        end = last and l == LAYERS - 1 and j == 3
                        split(nu - SHIFT * end)
                        pl.unit.n += SHIFT * end
                        residual(j * NB, j * 6, last)
                    if l == 0 and n == 0:
                        ada_part(6)

            dve.wait_ge(turned, 1)
            nc.vector.tensor_copy(ln_col[:, :, :, :].rearrange("p a l c -> p (a l c)"),
                                  ps[:, 4, 0:P])
            nc.vector.tensor_copy(adab_col[:, :, :].rearrange("p q c -> p (q c)"),
                                  ps[:, 4, P + 24:P + 24 + LAYERS * MODS * KC])
            nc.vector.tensor_copy(nrm_col[:, :], ps[:, 4, P:P + 24]).then_inc(turned_out, 1)
            pl.turn.n += 1

            dve.wait_ge(small_in, 16 * n_small)
            chain(nc.vector.tensor_copy(pos_f[:, :], pos_i[:, :]))
            for t in range(T):
                mark(nc.vector.tensor_scalar(ang[:, 0, t, :], inv[:, :], pos_f[:, t:t + 1], None,
                                             ALU.mult))
            own()
            whole = 1.5 * 2.0 ** 23
            chain(nc.vector.tensor_scalar(ang[:, 1, :, :], ang[:, 0, :, :],
                                          float(1 / (2 * np.pi)), None, ALU.mult))
            chain(nc.vector.tensor_scalar(ang[:, 1, :, :], ang[:, 1, :, :], whole, None, ALU.add))
            chain(nc.vector.tensor_scalar(ang[:, 1, :, :], ang[:, 1, :, :], -whole, None, ALU.add))
            for piece in two_pi_parts():
                chain(nc.vector.scalar_tensor_tensor(out=ang[:, 0, :, :], in0=ang[:, 1, :, :],
                                                     scalar=-piece, in1=ang[:, 0, :, :],
                                                     op0=ALU.mult, op1=ALU.add))
            chain(nc.vector.tensor_scalar(ang[:, 4, :, :], ang[:, 0, :, :], 3.1415925, -3.1415925,
                                          ALU.min, ALU.max))
            chain(nc.vector.tensor_scalar(ang[:, 2, :, :], ang[:, 4, :, :], -1.0, None, ALU.mult))
            chain(nc.vector.tensor_tensor(ang[:, 3, :, :], ang[:, 4, :, :], ang[:, 2, :, :],
                                          ALU.max))
            nc.vector.tensor_scalar(ang[:, 5, :, :], ang[:, 3, :, :], -1.0, float(np.pi / 2),
                                    ALU.mult, ALU.add).then_inc(angles, 1)

            dve.wait_ge(c_ready, 1)
            for j in range(QUARTERS):
                acc = gate[:, (j % 2) * 2 * NB:(j % 2 + 1) * 2 * NB]
                for k in range(KC):
                    pair = j * (KC // 2) + k // 2
                    slot = pair % FIRST_SLOTS
                    dve.wait_ge(first_in[slot], 32 * (pair // FIRST_SLOTS + 1))
                    w = first_w[:, slot, (k % 2) * 2 * NB:(k % 2 + 1) * 2 * NB]
                    if k == 0:
                        ins = nc.vector.tensor_scalar(acc, w, c_act[:, 0:1], None, ALU.mult)
                    else:
                        dve.wait_ge(first_mac, j * KC + k)
                        ins = nc.vector.scalar_tensor_tensor(out=acc, in0=w,
                                                             scalar=c_act[:, k:k + 1], in1=acc,
                                                             op0=ALU.mult, op1=ALU.add)
                    ins.then_inc(first_mac, 1)
                split(2 * QC // UC)
                dve.wait_ge(turned, pl.turn.at(1))
                cols = slice(j * QC, (j + 1) * QC)
                for q, plus, done in ((SH_A, 0.0, dve_step), (SC_A, 1.0, turned_out)):
                    nc.vector.scalar_tensor_tensor(
                        out=mod[:, q, cols], in0=ps[:, 4 + pl.turn.n % 2, q * QC:(q + 1) * QC],
                        scalar=plus, in1=adab_col[:, q, cols], op0=ALU.add, op1=ALU.add
                        ).then_inc(done, 1)
                pl.step.n += 1
                pl.turn.n += 1
                own()
                turns_written()
                nc.vector.tensor_copy(gcol[:, 0, cols], mod[:, SC_A, cols])
                nc.vector.tensor_copy(gcol[:, 1, cols], mod[:, SH_A, cols]).then_inc(gcol_ready, 1)
                turn_affine(hT_hi, hT_lo, QC // UC, j * QC // UC)
            split(SHIFT - QC // UC)
            latent(0)
            split(QC // UC)
            turn_affine(qlT_hi, qlT_lo, 2)
            latent(1)
            split(1)
            pl.block.n += 1
            for j in range(H * QH // NB):
                split(LORA // P // UC)
                pl.block.n += 1
                if j in (2, 3):
                    scale_xa(j - 2, None)
                if j == 0:
                    turn_affine(kvT_hi, kvT_lo, 2)
                    turn_copy(kpe[:, :, :].rearrange("p t e -> p (t e)"), lambda b: b[:, 0:T * ROPE])
                    turns_written()
            q_blocks = Count()
            q_blocks.n = pl.block.n
            dve.wait_ge(sincos, 1)
            for j in range(2 * D // NB):
                split(LORA // P // UC)
                pl.block.n += 1
                if j == 0:
                    for pair in range(2):
                        dve.wait_ge(pair_read[pair], pair_uses(q_blocks, pair))
                    k2 = kpe[:, :, :].rearrange("p t (f two) -> p t f two", two=2)
                    rope(k2[:, :, :, 0], k2[:, :, :, 1], cos[:, :, :], sin[:, :, :],
                         *(rope_t[:, n, 0:T, :] for n in range(4))).then_inc(q_roped, 1)
                    dve.wait_ge(q_roped, 1)
                if j in (2, 4):
                    t = (j - 2) // 2
                    q2 = mla_q[:, t, :].rearrange("p (h e) -> p h e", e=QH)[:, :, DH:QH]
                    q2 = q2.rearrange("p h (f two) -> p h f two", two=2)
                    cs, sn = (x[:, t, :].unsqueeze(1).to_broadcast([P, H, RH]) for x in (cos, sin))
                    rope(q2[:, :, :, 0], q2[:, :, :, 1], cs, sn,
                         *(rope_t[:, n, :, :] for n in range(4))).then_inc(q_roped, 1)
                    dve.wait_ge(q_roped, 2 + t)
            ada_part(G_A)
            turn_copy(kpT[:, :], lambda b: b[0:ROPE, 0:S])
            turns_written()
            attention(0, MLA_SCALE, mla_mask, True)
            w_o(0)
            layer_norm(0, (0, 0, 0, SH_F, SC_F))
            ffn(0)
            layer_norm(1, (2, 0, 1, SH_A, SC_A))

            turn_affine(hT_hi, hT_lo, KC // UC)
            split_scaling(1)
            split(KC // UC)
            pl.block.n += 2
            ada_part(8)
            split(1)
            block_done()
            pair = pl.block.n % 2
            f = [logf[:, n, :, :] for n in range(8)]
            nc.vector.tensor_copy(cumT[:, 0, :], ps[0:H, 2 * pair, 0:S]).then_inc(pair_read[pair], 1)
            pl.block.n += 1
            dve.wait_ge(turned, pl.turn.at(1))
            nc.vector.tensor_tensor(f[2], ps[:, 4 + pl.turn.n % 2, 0:T * H].rearrange(
                                        "p (t h) -> p t h", t=T),
                                    bf[:, :].unsqueeze(1).to_broadcast([P, T, H]), ALU.add
                                    ).then_inc(turned_out, 1)
            pl.turn.n += 1
            turns_written()
            chain(nc.vector.tensor_scalar(f[3], f[2], -1.0, None, ALU.mult))
            nc.vector.tensor_tensor(f[0], f[2], f[3], ALU.max).then_inc(logf_in, 1)
            mark(nc.vector.tensor_scalar(f[7], f[2], 0.0, None, ALU.min))
            dve.wait_ge(expf, 1)
            chain(nc.vector.tensor_scalar(f[3], f[1], 2.0, None, ALU.add))
            chain(nc.vector.reciprocal(f[5], f[3]))
            chain(nc.vector.tensor_tensor(f[4], f[1], f[5], ALU.mult))
            chain(nc.vector.tensor_tensor(f[5], f[4], f[4], ALU.mult))
            chain(nc.vector.tensor_scalar(f[6], f[5], 1.0 / 15, None, ALU.mult))
            for n in (13, 11, 9, 7, 5, 3):
                chain(nc.vector.scalar_tensor_tensor(out=f[6], in0=f[6], scalar=1.0 / n, in1=f[5],
                                                     op0=ALU.add, op1=ALU.mult))
            chain(nc.vector.scalar_tensor_tensor(out=f[6], in0=f[6], scalar=1.0, in1=f[4],
                                                 op0=ALU.add, op1=ALU.mult))
            nc.vector.scalar_tensor_tensor(out=f[7], in0=f[6], scalar=-2.0, in1=f[7],
                                           op0=ALU.mult, op1=ALU.add).then_inc(logf_ready, 1)

            def qkv(i):
                split(2 * KC // UC)
                pl.block.n += 2
            loop(dve, 5, pl, qkv, units=2 * KC // UC, blocks=2)
            ada_part(9)
            dve.wait_ge(turned, pl.turn.at(1))
            b = ps[0:H, 4 + pl.turn.n % 2, 0:S]
            nc.vector.tensor_scalar(cumT[:, 0, :], b, 1 / FOX_SCALE, None, ALU.mult)
            nc.vector.tensor_scalar(cumT[:, 1, :], b, -1 / FOX_SCALE, None, ALU.mult
                                    ).then_inc(turned_out, 1)
            pl.turn.n += 1
            attention(1, FOX_SCALE, fox_mask, False)
            w_o(1)
            layer_norm(2, (0, 1, 1, SH_F, SC_F))
            ffn(1)
            layer_norm(3)
            for t in range(T):
                scale_xa(t, 3, alpha=1.0)

        @block.tensor
        def _(pe):
            pl = Place()

            def bank_free():
                if pl.turn.i is not None or pl.turn.n >= 2:
                    pe.wait_ge(turned_out, pl.turn.at(-1))

            def turn(tile, c0=0):
                bank_free()
                for c in range(UC):
                    for t in range(T):
                        o = c * S + t * P
                        ins = nc.tensor.transpose(ps[:, 4 + pl.turn.n % 2, o:o + P],
                                                  tile(t, c0 + c), ident[:, :])
                ins.then_inc(turned, 1)
                pl.turn.n += 1

            def reduce_part(acc):
                bank_free()
                for j in range(KC):
                    ins = nc.tensor.matmul(ps[:, 4 + pl.turn.n % 2, j:j + 1],
                                           acc(j * P), ones[:, 0:1],
                                           start=True, stop=True)
                ins.then_inc(turned, 1)
                pl.turn.n += 1

            def reduce_pool(q):
                pe.wait_ge(pool_mac, KC * (POOL_PARTS.index(q) + 1))
                reduce_part(lambda o: ada_acc[:, o:o + P])

            def gate_turns(q):
                pe.wait_ge(turned_out, pl.turn.at())
                for j in range(4):
                    bank_free()
                    for c in range(4):
                        ins = nc.tensor.matmul(ps[:, 4 + pl.turn.n % 2, c * P:(c + 1) * P],
                                               mod[:, q, 4 * j + c:4 * j + c + 1].to_broadcast([P, P]),
                                               ident[:, :], start=True, stop=True)
                    ins.then_inc(turned, 1)
                    pl.turn.n += 1

            def narrow_products(width):
                pair = pl.block.n % 2
                pe.wait_ge(pair_read[pair], pair_uses(pl.block, pair))
                pe.wait_ge(lo_ready, pl.unit.at(1))
                s = pl.unit.n % RING
                o = ps[0:width, 2 * pair, 0:S]
                for c in range(KC):
                    w_hi, w_lo = (x[:, s, c * width:(c + 1) * width] for x in (whi, wlo))
                    nc.tensor.matmul(o, w_hi, hT_hi[:, c, :], start=(c == 0), stop=False)
                    nc.tensor.matmul(o, w_lo, hT_hi[:, c, :], start=False, stop=False)
                    ins = nc.tensor.matmul(o, w_hi, hT_lo[:, c, :], start=False, stop=(c == KC - 1))
                ins.then_inc(units_used, 1)
                pl.unit.n += 1
                pl.block.n += 1

            def turn_narrow(tile, width):
                bank_free()
                for t in range(T):
                    ins = nc.tensor.transpose(ps[:, 4 + pl.turn.n % 2, t * width:(t + 1) * width],
                                              tile[:, t * P:(t + 1) * P], ident[0:width, 0:width])
                ins.then_inc(turned, 1)
                pl.turn.n += 1

            def unit_products(pair, c0, chunks, hi, lo):
                pe.wait_ge(lo_ready, pl.unit.at(1))
                s = pl.unit.n % RING
                for c in range(UC):
                    w_hi, w_lo = (x[:, s, c * NB:(c + 1) * NB] for x in (whi, wlo))
                    for t in range(T):
                        a_hi, a_lo = (x[:, c0 + c, t * P:(t + 1) * P] for x in (hi, lo))
                        o = ps[:, 2 * pair + t, :]
                        first, end = c0 + c == 0, c0 + c == chunks - 1
                        nc.tensor.matmul(o, a_hi, w_hi, start=first, stop=False)
                        nc.tensor.matmul(o, a_hi, w_lo, start=False, stop=False)
                        ins = nc.tensor.matmul(o, a_lo, w_hi, start=False, stop=end)
                ins.then_inc(units_used, 1)
                pl.unit.n += 1

            def products(chunks, hi, lo, before_unit=None):
                pair = pl.block.n % 2
                if pl.block.n >= 2:
                    pe.wait_ge(pair_read[pair], pair_uses(pl.block, pair))
                for c0 in range(0, chunks, UC):
                    if before_unit is not None:
                        before_unit(c0 // UC)
                    unit_products(pair, c0, chunks, hi, lo)
                pl.block.n += 1

            def turned_products(tile):
                first = pl.turn.n

                def before(unit):
                    banks = range(0 if unit == 0 else 2 * unit + 1, 2 * unit + 3)
                    for b in banks:
                        if b < KC // UC:
                            turn(tile, UC * b)
                    pe.wait_ge(turned_out, first + unit + 1)
                products(KC, hT_hi, hT_lo, before_unit=before)

            def h_products():
                turned_products(lambda t, c: xa[:, t, c * P:(c + 1) * P])

            def attention(layer, q_tile, qpe_tile, k_tile, v_tile):
                g0 = H * layer
                pe.wait_ge(turned_out, pl.turn.at())
                for pair in range(2):
                    pe.wait_ge(pair_read[pair], pair_uses(pl.block, pair))
                for i in range(H + 3):
                    if i < H:
                        h, g = i, g0 + i
                        if g >= 2:
                            pe.wait_ge(qk_copied, g - 1)
                        for n, tile in enumerate((q_tile, k_tile)):
                            for t in range(T):
                                o = n * S + t * P
                                ins = nc.tensor.transpose(ps[:, g % 2, o:o + P], tile(t, h),
                                                          ident[:, :])
                        ins.then_inc(qk_turned, 1)
                    if 1 <= i <= H:
                        h, g = i - 1, g0 + i - 1
                        pe.wait_ge(qk_copied, g + 1)
                        if qpe_tile is not None:
                            pe.wait_ge(qp_copied, g + 1)
                        if g >= 2:
                            pe.wait_ge(masked, g - 1)
                        for t, a, n in ((0, 0, P), (1, P, S)):
                            o = ps[:, 2 + g % 2, a:a + n]
                            q = slice(t * P, (t + 1) * P)
                            nc.tensor.matmul(o, qkT[:, g % 2, q], qkT[:, g % 2, S:S + n],
                                             start=True, stop=False)
                            if qpe_tile is not None:
                                ins = nc.tensor.matmul(o, qpT[:, g % 2, q], kpT[:, 0:n],
                                                       start=False, stop=True)
                            else:
                                head = ident[0:H, h:h + 1]
                                nc.tensor.matmul(o, head.to_broadcast([H, P]), cumT[:, 1, 0:n],
                                                 start=False, stop=False)
                                ins = nc.tensor.matmul(o, cumT[:, 0, q], head.to_broadcast([H, n]),
                                                       start=False, stop=True)
                        ins.then_inc(scored, 1)
                    if 2 <= i <= H + 1:
                        g = g0 + i - 2
                        pe.wait_ge(exp_done, g + 1)
                        if g >= 2:
                            pe.wait_ge(pT_copied, g - 1)
                        for n in range(3):
                            ins = nc.tensor.transpose(ps[:, 4 + g % 2, n * P:(n + 1) * P],
                                                      p_sb[:, g % 2, n * P:(n + 1) * P], ident[:, :])
                        ins.then_inc(p_turned, 1)
                    if qpe_tile is not None and i < H:
                        if i >= 4:
                            pe.wait_ge(o_scaled, g0 + i - 3)
                        for t in range(T):
                            ins = nc.tensor.transpose(
                                ps[0:ROPE, 6 + (g0 + i) % 2, S + t * P:S + (t + 1) * P],
                                qpe_tile(t, i), ident[:, :])
                        ins.then_inc(qp_turned, 1)
                    if i >= 3:
                        h, g = i - 3, g0 + i - 3
                        pe.wait_ge(pT_copied, g + 1)
                        if g >= 2:
                            pe.wait_ge(o_scaled, g - 1)
                        for q_t, n, k_t in ((0, 0, 0), (1, 1, 0), (1, 2, 1)):
                            ins = nc.tensor.matmul(ps[:, 6 + g % 2, q_t * P:(q_t + 1) * P],
                                                   pT[:, g % 2, n * P:(n + 1) * P], v_tile(k_t, h),
                                                   start=(n < 2), stop=(n != 1))
                        ins.then_inc(pv_done, 1)

            def w_o(layer, o_tile):
                if layer == 0:
                    pe.wait_ge(early_mac, KC)
                    reduce_part(lambda o: gate[:, o:o + P])
                gate_turns(layer * MODS + G_A)
                pe.wait_ge(o_scaled, H * (layer + 1))
                turned_products(o_tile)
                products(KC, hT_hi, hT_lo)
                products(KC, hT_hi, hT_lo)
                products(KC, hT_hi, hT_lo)
                reduce_pool((SH_F, 10)[layer])

            def ffn(l):
                for n, nb in enumerate(FF_PASSES):
                    def turn_u():
                        pair = 1 - pl.block.n % 2
                        pe.wait_ge(pair_read[pair], pair_uses(pl.block, pair))
                        for b in range(2):
                            turn(lambda t, c: u[:, t, c * P:(c + 1) * P], UC * b)

                    def up(i, first=False):
                        if first and n == 0:
                            h_products()
                        else:
                            products(KC, hT_hi, hT_lo)
                        if not first:
                            pair = pl.block.n % 2
                            pe.wait_ge(pair_read[pair], pair_uses(pl.block, pair))
                            for b in range(2):
                                turn(lambda t, c: u[:, t, c * P:(c + 1) * P], UC * b)
                        products(KC, hT_hi, hT_lo)
                    if n == 0:
                        pe.wait_ge(norm_ready, 2 * l + 1)
                        pe.wait_ge(norm_act, 2 * l + 1)
                    up(0, first=True)
                    loop(pe, nb - 1, pl, up, units=2 * KC // UC, blocks=2, turns=2)

                    def before(unit):
                        if unit == 0 and part_in_down(l, n):
                            reduce_pool(l * MODS + G_F if n == 0 else 7)
                        if unit == 1:
                            turn_u()
                            u_turned.append(pl.turn.n)
                        if unit == 2 and n == 0:
                            gate_turns(l * MODS + G_F)
                        if unit == (4 * nb - 4) // UC:
                            pe.wait_ge(turned_out, u_turned[0])
                    u_turned = []
                    products(4 * nb, uT_hi, uT_lo, before_unit=before)
                    for _ in range(3):
                        products(4 * nb, uT_hi, uT_lo)
                    if l == 0 and n == 0:
                        reduce_pool(6)

            pe.wait_ge(small_in, 16 * n_small)
            pe.wait_ge(consts, n_consts)
            nc.tensor.transpose(ps[:, 4, 0:P], rows[:, 0, :], ident[:, :])
            nc.tensor.transpose(ps[:, 4, P:P + 24], rows[0:24, 1, :], ident[0:24, 0:24])
            n = MODS * KC
            for l in range(LAYERS):
                o = P + 24 + l * n
                ins = nc.tensor.transpose(ps[:, 4, o:o + n], rows[0:n, 2 + l, :], ident[0:n, 0:n])
            ins.then_inc(turned, 1)
            pl.turn.n += 1

            pe.wait_ge(x_in, 16)
            for j in range(QUARTERS):
                pe.wait_ge(first_mac, (j + 1) * KC)
                bank_free()
                for c in range(2 * QC):
                    o = (j % 2) * 2 * NB + c * P
                    ins = nc.tensor.matmul(ps[:, 4 + pl.turn.n % 2, c:c + 1], gate[:, o:o + P],
                                           ones[:, 0:1], start=True, stop=True)
                ins.then_inc(turned, 1)
                pl.turn.n += 1
                pe.wait_ge(gcol_ready, j + 1)
                first = pl.turn.n
                for c in range(j * QC, (j + 1) * QC, UC):
                    turn(lambda t, c: xa[:, t, c * P:(c + 1) * P], c)
                for pair in range(2):
                    for n in range(QC // UC):
                        pe.wait_ge(turned_out, first + n + 1)
                        unit_products(pair, j * QC + n * UC, KC, hT_hi, hT_lo)
            pl.block.n += 2

            def turn_latent(which):
                pe.wait_ge(pair_read[which], 1)
                for b in range(2):
                    turn(lambda t, c: lat[:, which, t, c * P:(c + 1) * P], UC * b)
            turn_latent(0)
            key_pair, key_reads = pl.block.n % 2, pair_uses(pl.block, pl.block.n % 2) + 1
            narrow_products(ROPE)
            for j in range(H * QH // NB):
                if j == 0:
                    pe.wait_ge(turned_out, pl.turn.at())
                products(LORA // P, qlT_hi, qlT_lo)
                if j == 0:
                    turn_latent(1)
                    pe.wait_ge(pair_read[key_pair], key_reads)
                    turn_narrow(kpT, ROPE)
            pe.wait_ge(turned_out, pl.turn.at())
            for j in range(2 * D // NB):
                products(LORA // P, kvT_hi, kvT_lo)
            reduce_pool(G_A)
            pe.wait_ge(q_roped, 3)
            bank_free()
            for t in range(T):
                ins = nc.tensor.transpose(ps[0:ROPE, 4 + pl.turn.n % 2, t * P:(t + 1) * P],
                                          kpe[:, t, :], ident[:, :])
            ins.then_inc(turned, 1)
            pl.turn.n += 1
            attention(0, lambda t, h: mla_q[:, t, h * QH:h * QH + DH],
                      lambda t, h: mla_q[:, t, h * QH + DH:(h + 1) * QH],
                      lambda t, h: mla_k[:, t, h * DH:(h + 1) * DH],
                      lambda t, h: mla_v[:, t, h * DH:(h + 1) * DH])
            w_o(0, lambda t, c: mla_v[:, t, c * P:(c + 1) * P])
            ffn(0)

            pe.wait_ge(norm_ready, 2)
            pe.wait_ge(norm_act, 2)
            h_products()
            products(KC, hT_hi, hT_lo)
            reduce_pool(8)
            pair, reads = pl.block.n % 2, pair_uses(pl.block, pl.block.n % 2) + 1
            narrow_products(H)
            pe.wait_ge(pair_read[pair], reads)
            turn_narrow(cumT[:, 0, :], H)

            def qkv(i):
                products(KC, hT_hi, hT_lo)
                products(KC, hT_hi, hT_lo)
            loop(pe, 5, pl, qkv, units=2 * KC // UC, blocks=2)
            reduce_pool(9)
            pe.wait_ge(logf_ready, 1)
            bank_free()
            nc.tensor.matmul(ps[0:H, 4 + pl.turn.n % 2, 0:S], logf[:, 7, 0, :], tri[:, :],
                             start=True, stop=False)
            nc.tensor.matmul(ps[0:H, 4 + pl.turn.n % 2, P:S], logf[:, 7, 1, :], tri[:, 0:P],
                             start=False, stop=True).then_inc(turned, 1)
            pl.turn.n += 1
            attention(1, lambda t, h: fox_qkv[:, t, h * DH:(h + 1) * DH], None,
                      lambda t, h: fox_qkv[:, t, D + h * DH:D + (h + 1) * DH],
                      lambda t, h: fox_qkv[:, t, 2 * D + h * DH:2 * D + (h + 1) * DH])
            w_o(1, lambda t, c: fox_qkv[:, t, 2 * D + c * P:2 * D + (c + 1) * P])
            ffn(1)


_INS = ["x", "c", "positions", "ada_w", "ada_b", "ln1_g", "ln1_b", "ln2_g", "ln2_b",
        "ffn_w1", "ffn_w3", "ffn_w2", "mla_w_down", "mla_q_norm", "mla_w_uq", "mla_kv_norm",
        "mla_w_uk", "mla_w_uv", "mla_w_o", "fox_w_in", "fox_b_f", "fox_w_o"]


def kernel(**inputs):
    from concourse.bacc import Bacc
    from concourse.bass_utils import run_bass_kernel_spmd

    nc = Bacc("TRN2", target_bir_lowering=False, num_devices=1)
    arrays = {name: np.ascontiguousarray(inputs[name]) for name in _INS}
    arrays["inv_freq"] = (np.float32(ROPE_THETA) ** (-np.arange(0, ROPE, 2, dtype=np.float32)
                                                     / np.float32(ROPE))).astype(np.float32)
    A = {name: nc.dram_tensor(f"in_{name}", a.shape, mybir.dt.from_np(a.dtype),
                              kind="ExternalInput").ap() for name, a in arrays.items()}
    out = nc.dram_tensor("out", (1, S, D), F32, kind="ExternalOutput").ap()
    trunk(nc, A, out)
    r = run_bass_kernel_spmd(nc, [{f"in_{n}": a for n, a in arrays.items()}], core_ids=[0])
    return r.results[0]["out"]
```
